# Optimizing a Trainium2 kernel written in Bass

```python
import jax
import jax.numpy as jnp
from jax import lax
import numpy as np

D_MODEL = 1024
BATCH = 1
SEQ = 256
DEPTH = 2

GRID_W = 64
CTX_LEN = 256
N_BRANCH = 4
BRANCH_W = 256
EPS = 1e-6

ML_HEADS = 4
ML_DH = BRANCH_W // ML_HEADS
ML_CHUNK = 128
ML_COLS = 4 * BRANCH_W + 4 * ML_HEADS

MLA_HEADS = 4
Q_LORA = 256
KV_LORA = 128
QK_NOPE = 64
QK_ROPE = 32
V_DIM = BRANCH_W // MLA_HEADS
ATT_BLOCK = 128
ROPE_THETA = 10000.0
MLA_COLS = Q_LORA + KV_LORA + QK_ROPE

POOL_WINDOWS = (2, 4, 8, 16)
POOL_GROUP = BRANCH_W // len(POOL_WINDOWS)
POOL_COLS = BRANCH_W

CONV_WIDTH = 3
CONV_COLS = 3 * BRANCH_W

IN_COLS = ML_COLS + MLA_COLS + POOL_COLS + CONV_COLS

N_EXPERTS = 64
TOP_K = 6
EXPERT_FF = 256
SHARED_FF = 256
ROUTE_SCALE = 2.5
MOE_BLOCK = 128

kernel_name = 'hybrid_gated_mlstm_mla_pool_conv_moe_dit'

def rms_norm(x, g):
    xf = x.astype(jnp.float32)
    y = xf * lax.rsqrt(jnp.mean(xf * xf, axis=-1, keepdims=True) + EPS)
    return (y * g.astype(jnp.float32)).astype(x.dtype)

def rope_angles(rows):
    row = jnp.repeat(jnp.arange(rows), GRID_W).astype(jnp.float32)
    col = jnp.tile(jnp.arange(GRID_W), rows).astype(jnp.float32)
    n_freq = QK_ROPE // 4
    inv = ROPE_THETA ** (-jnp.arange(n_freq, dtype=jnp.float32) / n_freq)
    return row[:, None] * inv, col[:, None] * inv

def rotate_half(x, ang):
    n = ang.shape[-1]
    cos = jnp.cos(ang)[None, :, None, :]
    sin = jnp.sin(ang)[None, :, None, :]
    x1, x2 = x[..., :n], x[..., n:]
    return jnp.concatenate([x1 * cos - x2 * sin, x2 * cos + x1 * sin], axis=-1).astype(x.dtype)

def axial_rope(x, ang):
    half = x.shape[-1] // 2
    return jnp.concatenate([rotate_half(x[..., :half], ang[0]), rotate_half(x[..., half:], ang[1])], axis=-1)

def mlstm_scan(q, k, v, li, lf, state, emit):
    bsz, nh, t_len, dh = q.shape
    n_chunks = t_len // ML_CHUNK

    def to_chunks(a):
        a = a.reshape(a.shape[:2] + (n_chunks, ML_CHUNK) + a.shape[3:])
        return jnp.moveaxis(a, 2, 0)

    tril = jnp.tril(jnp.ones((ML_CHUNK, ML_CHUNK), dtype=bool))

    def step(carry, inp):
        c_st, n_st, m_st = carry
        qc, kc, vc, lic, lfc = inp
        b = jnp.cumsum(lfc, axis=-1)
        b_end = b[..., -1]
        w_log = b_end[..., None] - b + lic
        m_new = jnp.maximum(b_end + m_st, jnp.max(w_log, axis=-1))
        decay = jnp.exp(b_end + m_st - m_new)
        w_s = jnp.exp(w_log - m_new[..., None])
        c_new = decay[..., None, None] * c_st + jnp.einsum('bhs,bhsd,bhse->bhde', w_s, kc, vc)
        n_new = decay[..., None] * n_st + jnp.einsum('bhs,bhsd->bhd', w_s, kc)
        if not emit:
            return (c_new, n_new, m_new), None
        d_log = jnp.where(tril, b[..., :, None] - b[..., None, :] + lic[..., None, :], -jnp.inf)
        inter = b + m_st[..., None]
        m_t = jnp.maximum(inter, jnp.max(d_log, axis=-1))
        a_inter = jnp.exp(inter - m_t)
        w_ts = jnp.exp(d_log - m_t[..., None]) * jnp.einsum('bhtd,bhsd->bhts', qc, kc)
        num = a_inter[..., None] * jnp.einsum('bhtd,bhde->bhte', qc, c_st) + jnp.einsum('bhts,bhse->bhte', w_ts, vc)
        den = a_inter * jnp.einsum('bhtd,bhd->bht', qc, n_st) + jnp.sum(w_ts, axis=-1)
        h = num / jnp.maximum(jnp.abs(den), jnp.exp(-m_t))[..., None]
        return (c_new, n_new, m_new), h

    state, hs = lax.scan(step, state, tuple(to_chunks(a) for a in (q, k, v, li, lf)))
    if not emit:
        return state, None
    return state, jnp.moveaxis(hs, 0, 2).reshape(bsz, nh, t_len, dh)

def mlstm_branch(p_lat, p_ctx, gate_bias, head_gain, emit_ctx):
    def prep(p):
        bsz, t_len, _ = p.shape
        q, k, v, o, g = jnp.split(p, [BRANCH_W, 2 * BRANCH_W, 3 * BRANCH_W, 4 * BRANCH_W], axis=-1)

        def heads(a):
            return a.reshape(bsz, t_len, ML_HEADS, ML_DH).transpose(0, 2, 1, 3).astype(jnp.float32)

        g = (g.astype(jnp.float32) + gate_bias).reshape(bsz, t_len, 4, ML_HEADS).transpose(2, 0, 3, 1)
        return heads(q), heads(k) * (ML_DH ** -0.5), heads(v), o, g

    ql, kl, vl, ol, gl = prep(p_lat)
    qc, kc, vc, oc, gc = prep(p_ctx)
    bsz = ql.shape[0]
    zero_state = (jnp.zeros((bsz, ML_HEADS, ML_DH, ML_DH), jnp.float32),
                  jnp.zeros((bsz, ML_HEADS, ML_DH), jnp.float32),
                  jnp.zeros((bsz, ML_HEADS), jnp.float32))
    h_lat, h_ctx = None, None
    for rev in (False, True):
        gi, gf = (2, 3) if rev else (0, 1)
        tf = (lambda a: jnp.flip(a, axis=2)) if rev else (lambda a: a)
        st_ctx, hc = mlstm_scan(tf(qc), tf(kc), tf(vc), tf(gc[gi]), tf(jax.nn.log_sigmoid(gc[gf])), zero_state, emit_ctx)
        _, hl = mlstm_scan(tf(ql), tf(kl), tf(vl), tf(gl[gi]), tf(jax.nn.log_sigmoid(gl[gf])), st_ctx, True)
        h_lat = tf(hl) if h_lat is None else h_lat + tf(hl)
        if emit_ctx:
            h_ctx = tf(hc) if h_ctx is None else h_ctx + tf(hc)

    def finish(h, o):
        bsz_, nh, t_len, dh = h.shape
        h = rms_norm(h.transpose(0, 2, 1, 3), head_gain.reshape(ML_HEADS, ML_DH)).reshape(bsz_, t_len, BRANCH_W)
        return (h * jax.nn.sigmoid(o.astype(jnp.float32))).astype(o.dtype)

    y_lat = finish(h_lat, ol)
    y_ctx = finish(h_ctx, oc) if emit_ctx else None
    return y_lat, y_ctx

def mla_project(p, ang, want_q, g_cq, g_ckv, w_uq, w_ukv, g_qn, g_kn):
    bsz, t_len, _ = p.shape
    cq, ckv, kr = jnp.split(p, [Q_LORA, Q_LORA + KV_LORA], axis=-1)
    kv = (rms_norm(ckv, g_ckv) @ w_ukv).reshape(bsz, t_len, MLA_HEADS, QK_NOPE + V_DIM)
    k_nope, v = kv[..., :QK_NOPE], kv[..., QK_NOPE:]
    k_rope = jnp.broadcast_to(kr[:, :, None, :], (bsz, t_len, MLA_HEADS, QK_ROPE))
    k = rms_norm(jnp.concatenate([k_nope, k_rope], axis=-1), g_kn)
    if ang is not None:
        k = jnp.concatenate([k[..., :QK_NOPE], axial_rope(k[..., QK_NOPE:], ang)], axis=-1)
    q = None
    if want_q:
        q = (rms_norm(cq, g_cq) @ w_uq).reshape(bsz, t_len, MLA_HEADS, QK_NOPE + QK_ROPE)
        q = rms_norm(q, g_qn)
        if ang is not None:
            q = jnp.concatenate([q[..., :QK_NOPE], axial_rope(q[..., QK_NOPE:], ang)], axis=-1)
    return q, k, v

def attend_blocks(q, k, v):
    bsz, tq, nh, dq = q.shape
    nb = tq // ATT_BLOCK
    qb = jnp.moveaxis(q.reshape(bsz, nb, ATT_BLOCK, nh, dq), 1, 0)
    scale = dq ** -0.5

    def one(q_blk):
        s = jnp.einsum('bqhd,bkhd->bhqk', q_blk, k, preferred_element_type=jnp.float32) * scale
        p = jax.nn.softmax(s, axis=-1).astype(v.dtype)
        return jnp.einsum('bhqk,bkhd->bqhd', p, v)

    out = lax.map(one, qb)
    return jnp.moveaxis(out, 0, 1).reshape(bsz, tq, nh, v.shape[-1])

def pool_mix(u, w_pool, pool_scale):
    bsz, t_len, cw = u.shape
    uf = u.astype(jnp.float32)
    cs = jnp.concatenate([jnp.zeros((bsz, 1, cw), jnp.float32), jnp.cumsum(uf, axis=1)], axis=1)
    t = jnp.arange(t_len)
    outs = []
    for gi, w in enumerate(POOL_WINDOWS):
        lo = jnp.clip(t - w // 2, 0, t_len)
        hi = jnp.clip(t + w // 2, 0, t_len)
        sl = slice(gi * POOL_GROUP, (gi + 1) * POOL_GROUP)
        seg = cs[:, :, sl]
        mean = (seg[:, hi] - seg[:, lo]) / (hi - lo).astype(jnp.float32)[None, :, None]
        outs.append(mean - uf[:, :, sl])
    y = jnp.stack(outs, axis=2)
    y = jnp.einsum('btgc,gcd->btgd', y, w_pool.astype(jnp.float32)).reshape(bsz, t_len, cw)
    return (y * pool_scale).astype(u.dtype)

def short_conv_mix(u, gate_b, gate_c, w_conv, b_conv):
    t_len = u.shape[1]
    pad = CONV_WIDTH // 2
    z = jnp.pad(gate_c * u, ((0, 0), (pad, pad), (0, 0)))
    y = b_conv
    for j in range(CONV_WIDTH):
        y = y + z[:, j:j + t_len] * w_conv[j]
    return gate_b * y

def gated_merge(h, ys, w_gate, b_gate, w_branch, w_out):
    acc = None
    for i, y in enumerate(ys):
        term = jax.nn.sigmoid(h @ w_gate[i] + b_gate[i]) * (y @ w_branch[i])
        acc = term if acc is None else acc + term
    return acc @ w_out

def moe_ffn(h, w_router, b_router, w1, w3, w2, ws1, ws3, ws2):
    n_tok, d = h.shape
    scores = jax.nn.sigmoid((h @ w_router).astype(jnp.float32))
    _, idx = lax.top_k(scores + b_router.astype(jnp.float32), TOP_K)
    s_sel = jnp.take_along_axis(scores, idx, axis=-1)
    wts = s_sel / jnp.sum(s_sel, axis=-1, keepdims=True) * ROUTE_SCALE

    n_assign = n_tok * TOP_K
    e_flat = idx.reshape(-1)
    tok_flat = jnp.repeat(jnp.arange(n_tok, dtype=jnp.int32), TOP_K)
    order = jnp.argsort(e_flat)
    e_s, tok_s, w_s = e_flat[order], tok_flat[order], wts.reshape(-1)[order]
    counts = jnp.bincount(e_flat, length=N_EXPERTS)
    padded = (counts + MOE_BLOCK - 1) // MOE_BLOCK * MOE_BLOCK
    pad_end = jnp.cumsum(padded)
    pad_start = pad_end - padded
    grp_start = jnp.cumsum(counts) - counts
    dest = pad_start[e_s] + (jnp.arange(n_assign) - grp_start[e_s])
    n_blocks = -(-n_assign // MOE_BLOCK) + N_EXPERTS
    n_rows = n_blocks * MOE_BLOCK
    row_tok = jnp.full((n_rows,), n_tok, jnp.int32).at[dest].set(tok_s)
    row_w = jnp.zeros((n_rows,), jnp.float32).at[dest].set(w_s)
    blk_e = jnp.clip(jnp.searchsorted(pad_end, jnp.arange(n_blocks) * MOE_BLOCK, side='right'), 0, N_EXPERTS - 1)
    h_pad = jnp.concatenate([h, jnp.zeros((1, d), h.dtype)], axis=0)

    def step(acc, inp):
        toks, wr, e = inp
        xb = h_pad[toks]
        a = jax.nn.silu(xb @ w1[e]) * (xb @ w3[e])
        yb = (a @ w2[e]) * wr[:, None]
        return acc.at[toks].add(yb.astype(jnp.float32)), None

    acc0 = jnp.zeros((n_tok + 1, d), jnp.float32)
    acc, _ = lax.scan(step, acc0, (row_tok.reshape(n_blocks, MOE_BLOCK), row_w.reshape(n_blocks, MOE_BLOCK), blk_e))
    shared = (jax.nn.silu(h @ ws1) * (h @ ws3)) @ ws2
    return (acc[:n_tok] + shared.astype(jnp.float32)).astype(h.dtype)

def hybrid_layer(x, ctx, c, c_ctx, ang, emit_ctx, lp):
    bsz, t_len, d = x.shape
    mod = (jax.nn.silu(c) @ lp['w_mod'] + lp['b_mod'])[:, None, :]
    mod_c = (jax.nn.silu(c_ctx) @ lp['w_mod'] + lp['b_mod'])[None, None, :]
    sh1, sc1, gt1, sh2, sc2, gt2 = jnp.split(mod, 6, axis=-1)
    csh1, csc1, cgt1, csh2, csc2, cgt2 = jnp.split(mod_c, 6, axis=-1)

    hx = rms_norm(x, lp['g_mix']) * (1 + sc1) + sh1
    hc = rms_norm(ctx, lp['g_mix']) * (1 + csc1) + csh1
    px = hx @ lp['w_in']
    pc = hc @ lp['w_in']
    cuts = [ML_COLS, ML_COLS + MLA_COLS, ML_COLS + MLA_COLS + POOL_COLS]
    ml_x, mla_x, pool_x, conv_x = jnp.split(px, cuts, axis=-1)
    ml_c, mla_c, pool_c, conv_c = jnp.split(pc, cuts, axis=-1)

    y_ml, yc_ml = mlstm_branch(ml_x, ml_c, lp['ml_gate_bias'], lp['ml_head_gain'], emit_ctx)

    mla_w = (lp['mla_g_cq'], lp['mla_g_ckv'], lp['mla_w_uq'], lp['mla_w_ukv'], lp['mla_g_qn'], lp['mla_g_kn'])
    q_l, k_l, v_l = mla_project(mla_x, ang, True, *mla_w)
    q_c, k_c, v_c = mla_project(mla_c, None, emit_ctx, *mla_w)
    k_all = jnp.concatenate([k_c, k_l], axis=1)
    v_all = jnp.concatenate([v_c, v_l], axis=1)
    y_mla = attend_blocks(q_l, k_all, v_all).reshape(bsz, t_len, BRANCH_W)

    y_pool = pool_mix(pool_x, lp['pool_w'], lp['pool_scale'])
    u_x, b_x, c_x = jnp.split(conv_x, 3, axis=-1)
    y_conv = short_conv_mix(u_x, b_x, c_x, lp['conv_w'], lp['conv_b'])

    merge_w = (lp['w_gate'], lp['b_gate'], lp['w_branch'], lp['w_out'])
    x = x + gt1 * gated_merge(hx, (y_ml, y_mla, y_pool, y_conv), *merge_w)
    if emit_ctx:
        yc_mla = attend_blocks(q_c, k_c, v_c).reshape(bsz, -1, BRANCH_W)
        yc_pool = pool_mix(pool_c, lp['pool_w'], lp['pool_scale'])
        u_c, b_c, c_c = jnp.split(conv_c, 3, axis=-1)
        yc_conv = short_conv_mix(u_c, b_c, c_c, lp['conv_w'], lp['conv_b'])
        ctx = ctx + cgt1 * gated_merge(hc, (yc_ml, yc_mla, yc_pool, yc_conv), *merge_w)

    hx2 = rms_norm(x, lp['g_ffn']) * (1 + sc2) + sh2
    tokens = hx2.reshape(-1, d)
    if emit_ctx:
        hc2 = rms_norm(ctx, lp['g_ffn']) * (1 + csc2) + csh2
        tokens = jnp.concatenate([tokens, hc2.reshape(-1, d)], axis=0)
    f = moe_ffn(tokens, lp['moe_w_router'], lp['moe_b_router'], lp['moe_w1'], lp['moe_w3'], lp['moe_w2'],
                lp['moe_ws1'], lp['moe_ws3'], lp['moe_ws2'])
    x = x + gt2 * f[:bsz * t_len].reshape(bsz, t_len, d)
    if emit_ctx:
        ctx = ctx + cgt2 * f[bsz * t_len:].reshape(ctx.shape)
    return x, ctx

def setup_inputs(seed: int = 0) -> dict:
    key = jax.random.key(seed)
    ks = iter(jax.random.split(key, 40))

    def nrm(shape, scale):
        return jax.random.normal(next(ks), shape, jnp.float32) * scale

    def gain(shape):
        return 1.0 + nrm(shape, 0.02)

    L, D = DEPTH, D_MODEL
    f_bias = jnp.linspace(3.0, 6.0, ML_HEADS, dtype=jnp.float32)
    z_bias = jnp.zeros((ML_HEADS,), jnp.float32)
    gate_base = jnp.concatenate([z_bias, f_bias, z_bias, f_bias])
    return {
        'x': nrm((BATCH, SEQ, D), 1.0),
        'c': nrm((BATCH, D), 1.0),
        'ctx': nrm((BATCH, CTX_LEN, D), 1.0),
        'c_ctx': nrm((D,), 1.0),
        'w_mod': nrm((L, D, 6 * D), 0.5 * D ** -0.5),
        'b_mod': nrm((L, 6 * D), 0.02),
        'g_mix': gain((L, D)),
        'g_ffn': gain((L, D)),
        'w_in': nrm((L, D, IN_COLS), D ** -0.5),
        'ml_gate_bias': gate_base + nrm((L, 4 * ML_HEADS), 0.1),
        'ml_head_gain': gain((L, BRANCH_W)),
        'mla_g_cq': gain((L, Q_LORA)),
        'mla_g_ckv': gain((L, KV_LORA)),
        'mla_w_uq': nrm((L, Q_LORA, MLA_HEADS * (QK_NOPE + QK_ROPE)), Q_LORA ** -0.5),
        'mla_w_ukv': nrm((L, KV_LORA, MLA_HEADS * (QK_NOPE + V_DIM)), KV_LORA ** -0.5),
        'mla_g_qn': gain((L, QK_NOPE + QK_ROPE)),
        'mla_g_kn': gain((L, QK_NOPE + QK_ROPE)),
        'pool_w': nrm((L, len(POOL_WINDOWS), POOL_GROUP, POOL_GROUP), POOL_GROUP ** -0.5),
        'pool_scale': gain((L, BRANCH_W)),
        'conv_w': nrm((L, CONV_WIDTH, BRANCH_W), CONV_WIDTH ** -0.5),
        'conv_b': nrm((L, BRANCH_W), 0.02),
        'w_gate': nrm((L, N_BRANCH, D, D), D ** -0.5),
        'b_gate': nrm((L, N_BRANCH, D), 0.02),
        'w_branch': nrm((L, N_BRANCH, BRANCH_W, D), BRANCH_W ** -0.5),
        'w_out': nrm((L, D, D), D ** -0.5),
        'moe_w_router': nrm((L, D, N_EXPERTS), D ** -0.5),
        'moe_b_router': nrm((L, N_EXPERTS), 0.01),
        'moe_w1': nrm((L, N_EXPERTS, D, EXPERT_FF), D ** -0.5),
        'moe_w3': nrm((L, N_EXPERTS, D, EXPERT_FF), D ** -0.5),
        'moe_w2': nrm((L, N_EXPERTS, EXPERT_FF, D), EXPERT_FF ** -0.5),
        'moe_ws1': nrm((L, D, SHARED_FF), D ** -0.5),
        'moe_ws3': nrm((L, D, SHARED_FF), D ** -0.5),
        'moe_ws2': nrm((L, SHARED_FF, D), SHARED_FF ** -0.5),
    }

def reference(x, c, ctx, c_ctx, w_mod, b_mod, g_mix, g_ffn, w_in, ml_gate_bias, ml_head_gain,
              mla_g_cq, mla_g_ckv, mla_w_uq, mla_w_ukv, mla_g_qn, mla_g_kn, pool_w, pool_scale,
              conv_w, conv_b, w_gate, b_gate, w_branch, w_out, moe_w_router, moe_b_router,
              moe_w1, moe_w3, moe_w2, moe_ws1, moe_ws3, moe_ws2):
    rows = x.shape[1] // GRID_W
    ang = rope_angles(rows)
    for l in range(DEPTH):
        emit_ctx = l < DEPTH - 1
        lp = {
            'w_mod': w_mod[l], 'b_mod': b_mod[l], 'g_mix': g_mix[l], 'g_ffn': g_ffn[l], 'w_in': w_in[l],
            'ml_gate_bias': ml_gate_bias[l], 'ml_head_gain': ml_head_gain[l],
            'mla_g_cq': mla_g_cq[l], 'mla_g_ckv': mla_g_ckv[l], 'mla_w_uq': mla_w_uq[l], 'mla_w_ukv': mla_w_ukv[l],
            'mla_g_qn': mla_g_qn[l], 'mla_g_kn': mla_g_kn[l],
            'pool_w': pool_w[l], 'pool_scale': pool_scale[l], 'conv_w': conv_w[l], 'conv_b': conv_b[l],
            'w_gate': w_gate[l], 'b_gate': b_gate[l], 'w_branch': w_branch[l], 'w_out': w_out[l],
            'moe_w_router': moe_w_router[l], 'moe_b_router': moe_b_router[l],
            'moe_w1': moe_w1[l], 'moe_w3': moe_w3[l], 'moe_w2': moe_w2[l],
            'moe_ws1': moe_ws1[l], 'moe_ws3': moe_ws3[l], 'moe_ws2': moe_ws2[l],
        }
        x, ctx = hybrid_layer(x, ctx, c, c_ctx, ang, emit_ctx, lp)
    return x


_drawn_inputs = setup_inputs


def setup_inputs(seed=0):
    import zlib

    import numpy as np

    out = dict(_drawn_inputs(seed))
    spreads = {}
    factors = {'ml_head_gain': 4.838,
     'mla_g_cq': 6.349,
     'mla_g_ckv': 4.961,
     'mla_g_qn': 5.526,
     'mla_g_kn': 6.559,
     'conv_b': 2.679,
     'b_gate': 4.138}
    for name, (base, spread) in spreads.items():
        noise = np.random.default_rng([zlib.crc32(name.encode()), seed]).standard_normal(out[name].shape)
        drawn = base * np.exp(spread * noise) if base else spread * noise
        out[name] = jnp.asarray(drawn.astype(out[name].dtype))
    for name, factor in factors.items():
        out[name] = (out[name] * factor).astype(out[name].dtype)
    return out
```

```python
from contextlib import ExitStack

import numpy as np

import concourse.bass as bass
from concourse import mybir

ALU = mybir.AluOpType
ACT = mybir.ActivationFunctionType
AX = mybir.AxisListType
F32 = mybir.dt.float32
I32 = mybir.dt.int32
U32 = mybir.dt.uint32

P = 128
D = 1024
KD = D // P
SEQ = 256
DEPTH = 2
EPS = 1e-6
HEADS = 4
DH = 64
QK = 96
ROPE = 32
NOPE = 64
BW = 256
FF = 256
NE = 64
TOPK = 6
ROUTE_SCALE = 2.5
GRID_W = 64
NT = 4
TOUT = (4, 2)
CAPS = (128, 64)
PASSES = 4
BIG = 1.0e6
NEG = -1.0e30

U_MOD, U_IN, U_GATE, U_OUT, U_SHARED, U_EXP = 0, 8, 12, 20, 22, 23
UNITS = U_EXP + NE
WSLOTS = 4
WLEN = 6144
MODC = 768
IN_UNITS = ((0, 768), (768, 1456), (1456, 2224), (2224, 2480))

IN_CHUNKS = ([(0, 128 * c, c >= 2) for c in range(6)] + [(1, 0, False), (1, 128, False)]
             + [(1, 272, False), (1, 400, False), (1, 528, True)]
             + [(2, 128 * c, False) for c in range(6)] + [(3, 0, False), (3, 128, False)])
C_Q, C_K, C_V, C_O, C_CQ, C_CKV, C_POOL, C_CONV = 0, 2, 4, 6, 8, 10, 11, 13
IN_G, IN_KR = 256, 656

R_BMOD, R_GMIX, R_GFFN, R_BGATE, R_HGAIN, R_PSCALE = 0, 48, 56, 64, 96, 98
R_CONVW, R_CONVB, R_GCQ, R_GCKV, R_C, R_CCTX, ROWS = 100, 106, 108, 110, 111, 119, 127
M_SH1, M_SC1, M_GT1, M_SH2, M_SC2, M_GT2 = 0, 8, 16, 24, 32, 40

K_ID, K_TF, K_TR, K_MF, K_MR, K_ONE, K_IOTA, K_TOK, K_RC, K_RS, K_EPS, K_END = (
    0, 128, 256, 384, 512, 640, 768, 896, 900, 964, 1028, 1029)

ORDER = ((2, 3, 0, 1), (3, 2, 1, 0))


class Signal:

    def __init__(self, sem, *per_layer):
        self.sem, self.per_layer = sem, per_layer

    def at(self, layer, n):
        return self.sem, sum(self.per_layer[:layer]) + n


def constants():
    c = np.zeros((P, K_END), np.float32)
    i = np.arange(P)
    c[:, K_ID:K_ID + P] = np.eye(P)
    c[:, K_TF:K_TF + P] = i[:, None] <= i[None, :]
    c[:, K_TR:K_TR + P] = i[:, None] >= i[None, :]
    c[:, K_MF:K_MF + P] = np.where(i[None, :] <= i[:, None], 0.0, NEG)
    c[:, K_MR:K_MR + P] = np.where(i[None, :] >= i[:, None], 0.0, NEG)
    c[:, K_ONE:K_ONE + P] = 1.0
    c[:, K_IOTA:K_IOTA + P] = i[None, :]
    c[:, K_TOK:K_TOK + 4] = i[:, None] + P * np.arange(4)[None, :]
    c[:, K_EPS] = EPS
    inv = np.float32(10000.0) ** (-np.arange(8, dtype=np.float32) / np.float32(8))
    for t in range(2):
        tok = t * P + i
        for half, pos in enumerate((tok // GRID_W, tok % GRID_W)):
            ang = pos.astype(np.float32)[:, None] * inv
            at = t * 32 + half * 16
            c[:, K_RC + at:K_RC + at + 8] = c[:, K_RC + at + 8:K_RC + at + 16] = np.cos(ang)
            c[:, K_RS + at:K_RS + at + 8] = -np.sin(ang)
            c[:, K_RS + at + 8:K_RS + at + 16] = np.sin(ang)
    t = np.arange(SEQ)
    inv_count = np.zeros((P, 2, SEQ), np.float32)
    for g, w in enumerate((2, 4, 8, 16)):
        n = np.minimum(t + w // 2, SEQ) - np.maximum(t - w // 2, 0)
        inv_count[(g % 2) * 64:(g % 2) * 64 + 64, g // 2, :] = 1.0 / n
    return c, inv_count.reshape(P, 2 * SEQ)


def build(nc, x, c, ctx_in, c_ctx, w_mod, b_mod, g_mix, g_ffn, w_in, ml_gate_bias, ml_head_gain, mla_g_cq,
          mla_g_ckv, mla_w_uq, mla_w_ukv, mla_g_qn, mla_g_kn, pool_w, pool_scale, conv_w, conv_b, w_gate, b_gate,
          w_branch, w_out, moe_w_router, moe_b_router, moe_w1, moe_w3, moe_w2, moe_ws1, moe_ws3, moe_ws2,
          consts, inv_count, out):
    with ExitStack() as stack:
        def sb(name, *shape, dt=F32):
            return stack.enter_context(nc.sbuf_tensor(name, [P, *shape], dt))

        def sem(name):
            return stack.enter_context(nc.semaphore(name))

        def signal(name, *per_layer):
            return Signal(sem(name), *per_layer)

        ring = sb("ring", WSLOTS, WLEN)
        res = sb("res", NT, D)
        hT = sb("hT", KD, NT * P)
        A = sb("A", 13 * 512)
        B = sb("B", 7296)
        Y = sb("Y", 8, 512)
        cst = sb("cst", K_END)
        par = sb("par", DEPTH, ROWS)
        row = sb("row", 272)
        mod = sb("mod", 48, 2)
        gain = sb("gain", 2, KD, 2)
        silu_c = sb("silu_c", 2, KD)
        sm = sb("sm", 656)
        bank = [stack.enter_context(nc.psum_tensor(f"bank{i}", [P, 512], F32)) for i in range(8)]

        h2_rows = nc.dram_tensor("h2_rows", (NT * P, D), F32).ap()
        y_rows = nc.dram_tensor("y_rows", (NT * P * TOPK, D), F32).ap()

        ident = cst[:, K_ID:K_ID + P]
        ones = cst[:, K_ONE:K_ONE + P]
        tri = (cst[:, K_TF:K_TF + P], cst[:, K_TR:K_TR + P])
        mask = (cst[:, K_MF:K_MF + P], cst[:, K_MR:K_MR + P])
        eps = cst[:, K_EPS:K_EPS + 1]

        pT = A[:, :].rearrange("p (n t) -> p n t", t=512)
        cv = B[:, 0:3072].rearrange("p (n t) -> p n t", t=512)
        xn1 = Y[:, :, :].rearrange("p a b -> p (a b)").rearrange("p (t d) -> p t d", d=D)
        xn2 = A[:, 0:NT * D].rearrange("p (t d) -> p t d", d=D)
        inv_cnt = B[:, 6784:7296].rearrange("p (c t) -> p c t", c=2)
        par_raw = B[:, 0:2 * P].rearrange("p (l n) -> p l n", l=2)
        b_gatebias, b_gqn, b_gkn, b_router = row[:, 0:16], row[:, 16:112], row[:, 112:208], row[:, 208:272]

        lg = sm[:, 0:64].rearrange("p (s d i h) -> p s d i h", s=4, d=2, i=2)
        lfm = sm[:, 64:96].rearrange("p (s d h) -> p s d h", s=4, d=2)
        sm32 = [sm[:, 96 + 32 * i:128 + 32 * i].rearrange("p (s n) -> p s n", s=4) for i in range(11)]
        cumf, endf, uu, umax, cmax, t_a, ebias, emt, a_int, decay, w_s = sm32
        m_st = sm[:, 448:488].rearrange("p (s n) -> p s n", s=5)
        krt = sm[:, 488:616].rearrange("p (t n) -> p t n", t=4)
        stat = sm[:, 616:640]
        asum = sm[:, 640:648].rearrange("p (n h) -> p n h", n=2)
        pool_mark = sm[:, 648:649]
        dm = B[:, 0:4096].rearrange("p (n h t) -> p n h t", n=8, h=4)
        ktok = B[:, 4096:5120].rearrange("p (t n) -> p t n", t=4)
        vaug = B[:, 5120:6160].rearrange("p (t h e) -> p t h e", t=4, h=4)
        ptm = B[:, 6160:6672].rearrange("p (h t) -> p h t", h=4)
        kw = B[:, 6672:6928]
        cstate = B[:, 6928:7188].rearrange("p (d n e) -> p d n e", d=2, n=2)
        dg = pT[:, C_POOL, :]
        pm = pT[:, C_POOL + 1, :].rearrange("p (h t) -> p h t", h=4)
        hsum = A[:, C_V * 512:(C_V + 2) * 512].rearrange("p (t h e) -> p t h e", t=4, h=4)
        num = Y[:, 0, 0:260].rearrange("p (h e) -> p h e", h=4)
        hd = Y[:, 1, 0:256].rearrange("p (h e) -> p h e", h=4)
        den = Y[:, 1, 256:260]
        hsq = Y[:, 2:4, :].rearrange("p a b -> p (a b)").rearrange("p (t h e) -> p t h e", t=4, h=4)
        hss = Y[:, 1, 272:288].rearrange("p (t h) -> p t h", t=4)
        padw = 272
        pad_u = B[:, 3072:3072 + 544].rearrange("p (s t) -> p s t", s=2)
        win_a = B[:, 3616:3616 + 544].rearrange("p (s t) -> p s t", s=2)
        win_b = B[:, 4160:4160 + 544].rearrange("p (s t) -> p s t", s=2)
        pad_z = B[:, 4704:4704 + 544].rearrange("p (s t) -> p s t", s=2)
        acc_c = B[:, 5248:5248 + 512]

        qT_a = B[:, 0:2048].rearrange("p (h t) -> p h t", h=4)
        kT_a = B[:, 2048:4096].rearrange("p (h t) -> p h t", h=4)
        v_a = B[:, 4096:5120].rearrange("p (t h e) -> p t h e", t=4, h=4)
        pa = B[:, 5120:6144].rearrange("p (n k) -> p n k", n=2)
        paT = B[:, 6144:7168].rearrange("p (n k) -> p n k", n=2)
        qk_t = A[:, 0:768].rearrange("p (n h e) -> p n h e", n=2, h=4)
        qk_s = A[:, 1024:1792].rearrange("p (n h e) -> p n h e", n=2, h=4)
        qk_r = A[:, 1792:2304].rearrange("p (n h e) -> p n h e", n=2, h=4)[:, :, :, 0:ROPE]
        y_a = A[:, 2560:2816]
        sq_c = Y[:, 2:4, :]
        sq_kv = B[:, 0:512]

        accT = A[:, 0:4096].rearrange("p (k t) -> p k t", k=KD)
        sg_m = A[:, 4096:5120].rearrange("p (n t) -> p n t", n=2)
        gt_b = Y[:, :, :].rearrange("p a b -> p (a b)").rearrange("p (g s d) -> p g s d", g=2, s=2)
        dgm = A[:, 5120:5632]
        upd = B[:, 0:1024].rearrange("p (n t) -> p n t", n=2)

        hrow = B[:, 1024:5120].rearrange("p (n d) -> p n d", n=4)
        sc_r = A[:, 4096:4352].rearrange("p (t e) -> p t e", t=4)
        sb_r = A[:, 4352:4416]
        mx8 = A[:, 4416:4424]
        ixf = A[:, 4424:4432]
        ix8 = A[:, 4432:4440].bitcast(U32)
        oh = A[:, 4480:4864].rearrange("p (j e) -> p j e", j=TOPK)
        oh2 = A[:, 4864:5248].rearrange("p (j e) -> p j e", j=TOPK)
        vj = A[:, 5248:5312]
        msk = A[:, 5312:5568].rearrange("p (t e) -> p t e", t=4)
        rank = A[:, 5568:5824].rearrange("p (t e) -> p t e", t=4)
        val = A[:, 5824:6336].rearrange("p (t e n) -> p t e n", t=4, n=2)
        wgt = A[:, 6336:6368].rearrange("p (t j) -> p t j", t=4)
        sumw = A[:, 6368:6370]
        tok6 = A[:, 6372:6376]
        cnt_f = A[:, 6376:6377]
        cnt_i = A[:, 6377:6378].bitcast(I32)
        jcol = A[:, 6380:6386]
        a_sh = A[:, 0:1024].rearrange("p (j t) -> p j t", j=2)
        sg_sh = A[:, 1024:2048].rearrange("p (j t) -> p j t", j=2)

        xg = B[:, 0:2048].rearrange("p (n d) -> p n d", n=2)
        xT = B[:, 2048:4096].rearrange("p (n d) -> p n d", n=2)
        ysb = B[:, 4096:5120]
        sel = B[:, 5120:6144].rearrange("p (n t) -> p n t", n=2)
        act_a = B[:, 6144:6656].rearrange("p (n t) -> p n t", n=2)
        sig_a = B[:, 6656:7168].rearrange("p (n t) -> p n t", n=2)
        idx_g = [B[:, 7168 + 2 * i:7169 + 2 * i].bitcast(U32) for i in range(4)]
        idx_s = [B[:, 7176 + 2 * i:7177 + 2 * i].bitcast(U32) for i in range(4)]
        tmp1 = B[:, 7184:7185]
        comb = B[:, 0:6144].rearrange("p (n j d) -> p n j d", n=2, j=TOPK)
        cacc = B[:, 6144:6656]

        weights_in = [sem(f"weights_in{s}") for s in range(WSLOTS)]
        in_const, in_res, in_par = sem("in_const"), sem("in_res"), sem("in_par")
        in_row, in_cnt = signal("in_row", 64, 64), signal("in_cnt", 16, 16)
        par_t, par_ok, sigc_ok, silc_ok = sem("par_t"), sem("par_ok"), sem("sigc_ok"), sem("silc_ok")
        mod_p = signal("mod_p", 8, 8)
        mod_ok = signal("mod_ok", 1, 1)
        ss_ok = signal("ss_ok", 2, 2)
        rt_ok = signal("rt_ok", 2, 2)
        xn_ok = signal("xn_ok", 2, 2)
        xn_t = signal("xn_t", 16, 16)
        hT_v = signal("hT_v", 8, 8)
        hT_a = signal("hT_a", 8, 8)
        win_p = signal("win_p", 19, 19)
        win_v = signal("win_v", 10, 10)
        win_a_ok = signal("win_a_ok", 9, 9)
        gk_p = signal("gk_p", 1, 1)
        lg_ok = signal("lg_ok", 1, 1)
        elf_ok = signal("elf_ok", 1, 1)
        lf_ok = signal("lf_ok", 1, 1)
        b_p = signal("b_p", 1, 1)
        pool_in = signal("pool_in", 1, 1)
        pool_p = signal("pool_p", 2, 2)
        pool_y = signal("pool_y", 2, 2)
        kv_p = signal("kv_p", 4, 4)
        kv_ok = signal("kv_ok", 4, 4)
        dg_ok = signal("dg_ok", 8, 8)
        ub_p = signal("ub_p", 8, 8)
        ub_used = signal("ub_used", 8, 8)
        mg_ok = signal("mg_ok", 1, 1)
        mx_ok = signal("mx_ok", 1, 1)
        N_EMIT = (8, 4)
        w_ok = signal("w_ok", *N_EMIT)
        s_p = signal("s_p", *N_EMIT)
        p_ok = signal("p_ok", *N_EMIT)
        pt_p = signal("pt_p", *N_EMIT)
        pt_ok = signal("pt_ok", *N_EMIT)
        av_p = signal("av_p", *N_EMIT)
        av_used = signal("av_used", *N_EMIT)
        kw_ok = signal("kw_ok", 6, 6)
        st_p = signal("st_p", 6, 6)
        c_ok = signal("c_ok", 6, 6)
        hss_ok, hrt_ok, hn_ok = signal("hss_ok", 1, 1), signal("hrt_ok", 1, 1), signal("hn_ok", 1, 1)
        sigo_ok = signal("sigo_ok", 1, 1)
        hn_p = signal("hn_p", *TOUT)
        yml_ok = signal("yml_ok", *TOUT)
        sqc_ok = signal("sqc_ok", 1, 1)
        ssc_p, rtc_ok, rsc_ok = signal("ssc_p", 1, 1), signal("rtc_ok", 1, 1), signal("rsc_ok", 1, 1)
        qk_p = signal("qk_p", 4, 4)
        qk_ok = signal("qk_ok", 4, 4)
        qss_ok, qrt_ok, qkn_ok = signal("qss_ok", 4, 4), signal("qrt_ok", 4, 4), signal("qkn_ok", 4, 4)
        qkt_p = signal("qkt_p", 4, 4)
        qT_ok = signal("qT_ok", *TOUT)
        kT_ok = signal("kT_ok", 4, 4)
        N_ATT = (16, 8)
        as_p, am_ok, ae_ok = signal("as_p", *N_ATT), signal("am_ok", *N_ATT), signal("ae_ok", *N_ATT)
        at_p, at_ok, aav_p = signal("at_p", *N_ATT), signal("at_ok", *N_ATT), signal("aav_p", *N_ATT)
        ya_ok, ya_p, yat_ok = signal("ya_ok", *TOUT), signal("ya_p", *TOUT), signal("yat_ok", *TOUT)
        conv_ok = signal("conv_ok", 1, 1)
        mgate_p, mgate_a = signal("mgate_p", 32, 32), signal("mgate_a", 32, 32)
        mprod_ok, empty_ok, hprod_ok = signal("mprod_ok", 32, 32), signal("empty_ok", NE, NE), signal("hprod_ok", NE, NE)
        mbr_p, macc_ok = signal("mbr_p", 32, 32), signal("macc_ok", 33, 33)
        gdg_ok, gb_p, gb_ok = signal("gdg_ok", 8, 8), signal("gb_p", 8, 8), signal("gb_ok", 8, 8)
        o_p, o_ok = signal("o_p", 8, 4), signal("o_ok", 8, 4)
        r_p, r_sc = signal("r_p", 1, 1), signal("r_sc", 1, 1)
        rb_p, rb_ok, h2_out = signal("rb_p", *TOUT), signal("rb_ok", *TOUT), signal("h2_out", 64, 32)
        msk_ok, rank_p, rank_ok = signal("msk_ok", 1, 1), signal("rank_p", 1, 1), signal("rank_ok", 1, 1)
        sh_p, sh_sig, sh_a, sh_y, sh_ok = (signal("sh_p", 2, 2), signal("sh_sig", 2, 2), signal("sh_a", 2, 2),
                                           signal("sh_y", 8, 4), signal("sh_ok", 8, 4))
        sel_ok, tbl_p, idx_ok = signal("sel_ok", NE, NE), signal("tbl_p", NE, NE), signal("idx_ok", NE, NE)
        rows_in = [signal(f"rows_in{i}", 16 * NE // 2, 16 * NE // 2) for i in range(2)]
        xt_p, xt_v, xt_a = signal("xt_p", NE, NE), signal("xt_v", NE, NE), signal("xt_a", NE, NE)
        h_p, h_sig, a_ok = signal("h_p", NE, NE), signal("h_sig", NE, NE), signal("a_ok", NE, NE)
        y_p, y_v, y_a_ok = signal("y_p", NE, NE), signal("y_v", NE, NE), signal("y_a_ok", NE, NE)
        y_out = signal("y_out", 16 * NE, 16 * NE)
        moe_done = signal("moe_done", 1, 1)
        comb_in = [signal(f"comb_in{i}", 64, 32) for i in range(2)]
        comb_used = signal("comb_used", 8, 4)
        res_ok = sem("res_ok")
        reached = sem("reached")
        out_done = sem("out_done")
        order_v, order_a = sem("order_v"), sem("order_a")
        OV = [[sem(f"ov{layer}_{n}") for n in ("w", "prod", "scan", "sel", "tbl", "idx", "rows", "xt", "xte", "h",
                                              "sig", "a", "y", "ye", "out")] for layer in range(DEPTH)]

        ARRIVED = 64

        def weights_at(n):
            return weights_in[n % WSLOTS], ARRIVED * (n // WSLOTS + 1)

        def expert_of(w, layer, e):
            return w[layer, e] if isinstance(e, int) else w[layer, bass.ds(e, 1)].squeeze(0)

        def at_expert(table, t, e):
            if isinstance(e, int):
                return table[:, t, e]
            return table[:, t, bass.ds(e, 1)].squeeze(1)

        def two_before(i, at):
            return i * 16 + at if at >= 2 else i * (15 + at) + 1

        def w_slot(n):
            return ring[:, n % WSLOTS, :]

        def emits(layer, s):
            return layer == 0 or s >= 2

        def row_groups(layer):
            return ((0, 256), (256, 256))[:2 if layer == 0 else 1]

        def gate_steps(layer):
            return [(s, d) for s in range(4) for d in range(2)]

        block = stack.enter_context(nc.Block())

        @block.sync
        def _(sp):
            def unit_used(layer, u):
                if u < U_IN:
                    return mod_p.at(layer, u + 1)
                if u < U_GATE:
                    return (win_p.at(layer, 6), gk_p.at(layer, 1), win_p.at(layer, 17), qk_p.at(layer, 4))[u - U_IN]
                if u < U_OUT:
                    return mbr_p.at(layer, 4 * (u - U_GATE + 1))
                if u < U_SHARED:
                    return o_p.at(layer, TOUT[layer]) if u == U_OUT else r_p.at(layer, 1)
                if u < U_EXP:
                    return sh_y.at(layer, 2 * TOUT[layer])
                return y_p.at(layer, u - U_EXP + 1)

            def slot_free(n):
                if n >= WSLOTS:
                    m = n - WSLOTS
                    sp.wait_ge(*unit_used(m // UNITS, m % UNITS))

            def expert_load(dst, w1, w3, w2, done):
                sp.dma_start(dst[:, 0:2048], w1.rearrange("(p k) f -> p (k f)", p=P)).then_inc(done, 16)
                sp.dma_start(dst[:, 2048:4096], w3.rearrange("(p k) f -> p (k f)", p=P)).then_inc(done, 16)
                sp.dma_start(dst[:, 4096:6144].rearrange("p (j d) -> p j d", j=2),
                             w2.rearrange("(j p) d -> p j d", p=P)).then_inc(done, 32)

            for layer in range(DEPTH):
                base = layer * UNITS
                for u in range(8):
                    n = base + U_MOD + u
                    slot_free(n)
                    sp.dma_start(w_slot(n).rearrange("p (k c) -> p k c", k=KD),
                                 w_mod[layer, :, u * MODC:(u + 1) * MODC].rearrange("(k p) c -> p k c", p=P)
                                 ).then_inc(weights_in[n % WSLOTS], ARRIVED)
                for u, (c0, c1) in enumerate(IN_UNITS):
                    n = base + U_IN + u
                    slot_free(n)
                    sp.dma_start(w_slot(n)[:, 0:KD * (c1 - c0)].rearrange("p (k c) -> p k c", k=KD),
                                 w_in[layer, :, c0:c1].rearrange("(k p) c -> p k c", p=P)
                                 ).then_inc(weights_in[n % WSLOTS], ARRIVED if u < 3 else 16)
                    if u == 3:
                        s = w_slot(n)
                        sp.dma_start(s[:, 2048:2816].rearrange("p (c n) -> p c n", c=2),
                                     mla_w_uq[layer].rearrange("(c p) n -> p c n", p=P)
                                     ).then_inc(weights_in[n % WSLOTS], 16)
                        sp.dma_start(s[:, 2816:3328], mla_w_ukv[layer]).then_inc(weights_in[n % WSLOTS], 16)
                        sp.dma_start(s[:, 3328:3456].rearrange("p (g n) -> p g n", g=2),
                                     pool_w[layer].rearrange("(g a) c n -> (a c) g n", a=2)
                                     ).then_inc(weights_in[n % WSLOTS], 16)
                for u in range(8):
                    n = base + U_GATE + u
                    slot_free(n)
                    i, half = u // 2, u % 2
                    sp.dma_start(w_slot(n)[:, 0:4096].rearrange("p (k c) -> p k c", k=KD),
                                 w_gate[layer, i, :, half * 512:(half + 1) * 512].rearrange("(k p) c -> p k c", p=P)
                                 ).then_inc(weights_in[n % WSLOTS], 48)
                    sp.dma_start(w_slot(n)[:, 4096:5120].rearrange("p (k c) -> p k c", k=2),
                                 w_branch[layer, i, :, half * 512:(half + 1) * 512].rearrange("(k p) c -> p k c", p=P)
                                 ).then_inc(weights_in[n % WSLOTS], 16)
                for u in range(2):
                    n = base + U_OUT + u
                    slot_free(n)
                    sp.dma_start(w_slot(n)[:, 0:4096].rearrange("p (k c) -> p k c", k=KD),
                                 w_out[layer, :, u * 512:(u + 1) * 512].rearrange("(k p) c -> p k c", p=P)
                                 ).then_inc(weights_in[n % WSLOTS], ARRIVED if u == 0 else 48)
                    if u == 1:
                        sp.dma_start(w_slot(n)[:, 4096:4608].rearrange("p (k c) -> p k c", k=KD),
                                     moe_w_router[layer].rearrange("(k p) c -> p k c", p=P)
                                     ).then_inc(weights_in[n % WSLOTS], 16)
                n = base + U_SHARED
                slot_free(n)
                s = w_slot(n)
                for j, w in enumerate((moe_ws1, moe_ws3)):
                    sp.dma_start(s[:, 2048 * j:2048 * j + 2048].rearrange("p (k c) -> p k c", k=KD),
                                 w[layer].rearrange("(k p) c -> p k c", p=P)).then_inc(weights_in[n % WSLOTS], 16)
                sp.dma_start(s[:, 4096:6144].rearrange("p (j d) -> p j d", j=2),
                             moe_ws2[layer].rearrange("(j p) d -> p j d", p=P)).then_inc(weights_in[n % WSLOTS], 32)
                def load_experts(g):
                    for j in range(4):
                        n = base + U_EXP + j
                        e = g * 4 + j
                        if isinstance(g, int):
                            slot_free(n)
                        else:
                            sp.wait_ge(y_p.sem, e + (layer * NE - WSLOTS + 1))
                        expert_load(w_slot(n), expert_of(moe_w1, layer, e), expert_of(moe_w3, layer, e),
                                    expert_of(moe_w2, layer, e), weights_in[n % WSLOTS])

                load_experts(0)
                with sp.Fori(1, NE // 4) as g:
                    load_experts(g)
                w, y = OV[layer][0], OV[layer][12]
                sp.wait_ge(*rank_ok.at(layer, 1))
                sp.wait_ge(*y_p.at(layer, NE))
                most = sp.value_load(cnt_i[0:1, :], min_val=0, max_val=NT * P)
                with sp.Fori(1, PASSES) as q:
                    with sp.If(most > q * CAPS[layer]):
                        with sp.Fori(0, NE) as e:
                            sp.wait_ge(y, (q - 1) * NE + e + 1)
                            expert_load(ring[:, 0, :], expert_of(moe_w1, layer, e), expert_of(moe_w3, layer, e),
                                        expert_of(moe_w2, layer, e), w)
                        sp.wait_ge(y, q * NE + 1)
                        sp.sem_inc(reached, 1)

        @block.tensor
        def _(pe):
            mm = nc.tensor.matmul

            def w_need(n):
                pe.wait_ge(*weights_at(n))

            pe.wait_ge(in_const, 16)
            pe.wait_ge(in_par, 16 * 24)
            for layer in range(DEPTH):
                nc.tensor.transpose(bank[6][:, layer * P:layer * P + ROWS], par_raw[0:ROWS, layer, :],
                                    ident[0:ROWS, 0:ROWS]).then_inc(par_t, 1)

            def modulation(layer):
                base = layer * UNITS
                if layer == 0:
                    pe.wait_ge(silc_ok, 1)
                with pe.Fori(0, 2) as i:
                    for j in range(4):
                        n = base + U_MOD + j
                        pe.wait_ge(weights_in[n % WSLOTS], i * ARRIVED + ARRIVED * (n // WSLOTS + 1))
                        w = w_slot(n).rearrange("p (k c) -> p k c", k=KD)
                        for ch in range(6):
                            for k in range(KD):
                                last = mm(bank[7][:, bass.ds(i * 48 + (j * 12 + ch * 2), 2)],
                                          w[:, k, ch * P:(ch + 1) * P], silu_c[:, :, k],
                                          start=(k == 0), stop=(k == KD - 1))
                        last.then_inc(mod_p.sem, 1)

            def norm_transposes(layer, which):
                tiles = NT if which == 0 else TOUT[layer]
                src = xn1 if which == 0 else xn2
                pe.wait_ge(*xn_ok.at(layer, which + 1))
                for k in range(KD):
                    if k >= 2:
                        pe.wait_ge(*(hT_v if k % 2 == 0 else hT_a).at(layer, which * 4 + k // 2))
                    for t in range(tiles):
                        last = nc.tensor.transpose(bank[k % 2][:, t * P:(t + 1) * P], src[:, t, k * P:(k + 1) * P],
                                                   ident)
                    last.then_inc(xn_t.sem, 1)
                pe.wait_ge(*hT_v.at(layer, which * 4 + 4))
                pe.wait_ge(*hT_a.at(layer, which * 4 + 4))

            def input_projection(layer):
                base = layer * UNITS
                unit = -1
                for n, (u, col, ctx_too) in enumerate(IN_CHUNKS):
                    if u != unit:
                        w_need(base + U_IN + u)
                        unit = u
                        width = IN_UNITS[u][1] - IN_UNITS[u][0]
                        w = w_slot(base + U_IN + u)[:, 0:KD * width].rearrange("p (k c) -> p k c", k=KD)
                    size = 512 if layer == 0 or ctx_too else 256
                    if n >= 4:
                        pe.wait_ge(*(win_v if n % 2 == 0 else win_a_ok).at(layer, (n - 4) // 2 + 1))
                    for k in range(KD):
                        last = mm(bank[n % 4][:, 0:size], w[:, k, col:col + P], hT[:, k, 0:size],
                                  start=(k == 0), stop=(k == KD - 1))
                    last.then_inc(win_p.sem, 1)
                    if n == C_CKV:
                        for t in range(NT):
                            for at, c0, cols in ((0, IN_G, 16), (16, IN_KR, ROPE)):
                                for k in range(KD):
                                    last = mm(bank[4][:, t * 64 + at:t * 64 + at + cols], hT[:, k, t * P:(t + 1) * P],
                                              w[:, k, c0:c0 + cols], start=(k == 0), stop=(k == KD - 1))
                        last.then_inc(gk_p.sem, 1)

            def pool_branch(layer):
                size = TOUT[layer] * P
                w = w_slot(layer * UNITS + U_IN + 3)[:, 3328:3456].rearrange("p (g n) -> p g n", g=2)
                pe.wait_ge(*pool_in.at(layer, 1))
                for c in range(2):
                    for a in range(2):
                        if c == 1:
                            pe.wait_ge(*pool_y.at(layer, 1))
                        q = slice(a * 64, a * 64 + 64)
                        last = mm(bank[a][q, 0:size], w[q, c, :], pT[q, C_POOL + c, 0:size], start=True, stop=True)
                    last.then_inc(pool_p.sem, 1)

            def mlstm(layer):
                for t in range(NT):
                    if t >= 2:
                        pe.wait_ge(*kv_ok.at(layer, t - 1))
                    for c in range(4):
                        last = nc.tensor.transpose(bank[5 + t % 2][:, c * P:(c + 1) * P],
                                                   pT[:, C_K + c, t * P:(t + 1) * P], ident)
                    last.then_inc(kv_p.sem, 1)
                pe.wait_ge(*lf_ok.at(layer, 1))
                for s, d in gate_steps(layer):
                    at = s * 8 + d * 4
                    mm(bank[4][:, at:at + 4], tri[d], lfm[:, s, d, :], start=True, stop=True)
                last = mm(bank[4][:, 32:64], ones, lfm[:, :, :, :].rearrange("p s d h -> p (s d h)"),
                          start=True, stop=True)
                last.then_inc(b_p.sem, 1)
                pe.wait_ge(*pool_y.at(layer, 2))
                for n in range(8):
                    pe.wait_ge(*dg_ok.at(layer, n + 1))
                    if n >= 2:
                        pe.wait_ge(*ub_used.at(layer, n - 1))
                    mm(bank[n % 2][:, :], ones, dg, start=True, stop=True).then_inc(ub_p.sem, 1)
                pe.wait_ge(*ub_used.at(layer, 8))
                e = st = 0
                for s, d in gate_steps(layer):
                    t = ORDER[d][s]
                    tok = slice(t * P, (t + 1) * P)
                    if emits(layer, s):
                        e += 1
                        if e >= 2:
                            pe.wait_ge(*p_ok.at(layer, e - 1))
                        for h in range(HEADS):
                            q = slice((h % 2) * 64, (h % 2) * 64 + 64)
                            last = mm(bank[h % 2][:, (h // 2) * P:(h // 2 + 1) * P], pT[q, C_Q + h // 2, tok],
                                      pT[q, C_K + h // 2, tok], start=True, stop=True)
                        last.then_inc(s_p.sem, 1)
                        if s > 0:
                            pe.wait_ge(*c_ok.at(layer, (s - 1) * 2 + d + 1))
                            if e >= 2:
                                pe.wait_ge(*av_used.at(layer, e - 1))
                            for h in range(HEADS):
                                q = slice((h % 2) * 64, (h % 2) * 64 + 64)
                                mm(bank[4 + h % 2][:, (h // 2) * 65:(h // 2) * 65 + 65], pT[q, C_Q + h // 2, tok],
                                   cstate[q, d, h // 2, :], start=True, stop=True)
                        pe.wait_ge(*p_ok.at(layer, e))
                        if e >= 2:
                            pe.wait_ge(*pt_ok.at(layer, e - 1))
                        for h in range(HEADS):
                            last = nc.tensor.transpose(bank[2][:, h * P:(h + 1) * P], pm[:, h, :], ident)
                        last.then_inc(pt_p.sem, 1)
                        pe.wait_ge(*pt_ok.at(layer, e))
                        if e >= 2:
                            pe.wait_ge(*av_used.at(layer, e - 1))
                        for h in range(HEADS):
                            last = mm(bank[3][:, h * 65:h * 65 + 65], ptm[:, h, :], vaug[:, t, h, :],
                                      start=True, stop=True)
                        last.then_inc(av_p.sem, 1)
                    if s < 3:
                        st += 1
                        pe.wait_ge(*kw_ok.at(layer, st))
                        if st >= 2:
                            pe.wait_ge(*c_ok.at(layer, st - 1))
                        for n in range(2):
                            last = mm(bank[6][:, n * 130:n * 130 + 130], kw[:, n * P:(n + 1) * P],
                                      vaug[:, t, 2 * n:2 * n + 2, :].rearrange("p h e -> p (h e)"),
                                      start=True, stop=True)
                        last.then_inc(st_p.sem, 1)
                pe.wait_ge(*hn_ok.at(layer, 1))
                for t in range(TOUT[layer]):
                    if t >= 2:
                        pe.wait_ge(*yml_ok.at(layer, t - 1))
                    for c in range(2):
                        last = nc.tensor.transpose(bank[t % 2][:, c * P:(c + 1) * P],
                                                   hsum[:, t, 2 * c:2 * c + 2, :].rearrange("p h e -> p (h e)"), ident)
                    last.then_inc(hn_p.sem, 1)

            def latent_attention(layer):
                w = w_slot(layer * UNITS + U_IN + 3)
                w_uq = w[:, 2048:2816].rearrange("p (c n) -> p c n", c=2)
                w_ukv = w[:, 2816:3328]
                pe.wait_ge(*sqc_ok.at(layer, 1))
                for t in range(NT):
                    tok = slice(t * P, (t + 1) * P)
                    if t < TOUT[layer]:
                        for c in range(2):
                            mm(bank[4][:, 2 * t:2 * t + 1], sq_c[:, c, tok], ones[:, 0:1], start=(c == 0), stop=(c == 1))
                    last = mm(bank[4][:, 2 * t + 1:2 * t + 2], sq_kv[:, tok], ones[:, 0:1], start=True, stop=True)
                last.then_inc(ssc_p.sem, 1)
                pe.wait_ge(*yml_ok.at(layer, TOUT[layer]))
                for t in range(NT):
                    tok = slice(t * P, (t + 1) * P)
                    if t >= 1:
                        pe.wait_ge(*qk_ok.at(layer, t))
                    if t < TOUT[layer]:
                        for c in range(2):
                            mm(bank[0][:, 0:384], pT[:, C_CQ + c, tok], w_uq[:, c, :], start=(c == 0), stop=(c == 1))
                    mm(bank[1][:, :], pT[:, C_CKV, tok], w_ukv, start=True, stop=True).then_inc(qk_p.sem, 1)
                    pe.wait_ge(*qkn_ok.at(layer, t + 1))
                    if t >= 1:
                        pe.wait_ge(*kT_ok.at(layer, t))
                        pe.wait_ge(*qT_ok.at(layer, min(t, TOUT[layer])))
                    for n in range(2):
                        if n == 0 and t >= TOUT[layer]:
                            continue
                        for h in range(HEADS):
                            last = nc.tensor.transpose(bank[2 + n][0:QK, h * P:(h + 1) * P], qk_t[:, n, h, :], ident)
                    last.then_inc(qkt_p.sem, 1)
                last = None
                pe.wait_ge(*kT_ok.at(layer, NT))
                pe.wait_ge(*qT_ok.at(layer, TOUT[layer]))
                pairs = [(t, h) for t in range(TOUT[layer]) for h in range(HEADS)]

                def scores(n):
                    t, h = pairs[n]
                    k0 = 0 if t < 2 else 256
                    if n >= 2:
                        pe.wait_ge(*ae_ok.at(layer, n - 1))
                    mm(bank[5 + n % 2][:, 0:512 - k0], qT_a[0:QK, h, t * P:(t + 1) * P], kT_a[0:QK, h, k0:512],
                       start=True, stop=True).then_inc(as_p.sem, 1)

                def weighted_values(n):
                    t, h = pairs[n]
                    tiles = range(0 if t < 2 else 2, 4)
                    pe.wait_ge(*ae_ok.at(layer, n + 1))
                    if n >= 2:
                        pe.wait_ge(*at_ok.at(layer, n - 1))
                    for i, kt in enumerate(tiles):
                        last = nc.tensor.transpose(bank[2 + n % 2][:, i * P:(i + 1) * P], pa[:, n % 2, i * P:(i + 1) * P],
                                                   ident)
                    last.then_inc(at_p.sem, 1)
                    pe.wait_ge(*at_ok.at(layer, n + 1))
                    if h == 0 and t >= 1:
                        pe.wait_ge(*ya_ok.at(layer, t))
                    for i, kt in enumerate(tiles):
                        last = mm(bank[7][:, h * 64:(h + 1) * 64], paT[:, n % 2, i * P:(i + 1) * P], v_a[:, kt, h, :],
                                  start=(i == 0), stop=(i == len(tiles) - 1))
                    last.then_inc(aav_p.sem, 1)
                    if h == HEADS - 1:
                        pe.wait_ge(*ya_ok.at(layer, t + 1))
                        if t >= 1:
                            pe.wait_ge(*yat_ok.at(layer, t))
                        for c in range(2):
                            last = nc.tensor.transpose(bank[4][:, c * P:(c + 1) * P], y_a[:, c * P:(c + 1) * P], ident)
                        last.then_inc(ya_p.sem, 1)

                for n in range(len(pairs) + 1):
                    if n < len(pairs):
                        scores(n)
                    if n >= 1:
                        weighted_values(n - 1)

            def merge(layer):
                base = layer * UNITS + U_GATE
                size = TOUT[layer] * P
                pe.wait_ge(*yat_ok.at(layer, TOUT[layer]))
                pe.wait_ge(*conv_ok.at(layer, 1))
                pe.wait_ge(*macc_ok.at(layer, 1))
                with pe.Fori(0, 2) as i:
                    for j in range(4):
                        n = base + j
                        pe.wait_ge(weights_in[n % WSLOTS], i * ARRIVED + ARRIVED * (n // WSLOTS + 1))
                        wg = w_slot(n)[:, 0:4096].rearrange("p (k c) -> p k c", k=KD)
                        wb = w_slot(n)[:, 4096:5120].rearrange("p (k c) -> p k c", k=2)
                        for c in range(4):
                            at = 4 * j + c
                            pe.wait_ge(macc_ok.sem, two_before(i, at) + 33 * layer)
                            for k in range(KD):
                                last = mm(bank[c % 2][:, 0:size], wg[:, k, c * P:(c + 1) * P], hT[:, k, 0:size],
                                          start=(k == 0), stop=(k == KD - 1))
                            last.then_inc(mgate_p.sem, 1)
                            for k in range(2):
                                last = mm(bank[2 + c % 2][:, 0:size], wb[:, k, c * P:(c + 1) * P],
                                          Y[:, bass.ds(i * 4 + (j // 2 * 2 + k), 1), 0:size].squeeze(1),
                                          start=(k == 0), stop=(k == 1))
                            last.then_inc(mbr_p.sem, 1)

            def output_projection(layer):
                base = layer * UNITS + U_OUT
                sizes = len(row_groups(layer))
                n = 0
                for g in range(2):
                    for s in range(sizes):
                        for half in range(2):
                            n += 1
                            pe.wait_ge(*gdg_ok.at(layer, n))
                            if n >= 3:
                                pe.wait_ge(*gb_ok.at(layer, n - 2))
                            mm(bank[4 + n % 2][:, :], ones, dgm, start=True, stop=True).then_inc(gb_p.sem, 1)
                pe.wait_ge(*macc_ok.at(layer, 33))
                e = 0
                for u in range(2):
                    w_need(base + u)
                    w = w_slot(base + u)[:, 0:4096].rearrange("p (k c) -> p k c", k=KD)
                    for t in range(TOUT[layer]):
                        e += 1
                        if e >= 3:
                            pe.wait_ge(*o_ok.at(layer, e - 2))
                        for k in range(KD):
                            last = mm(bank[e % 2][:, :], accT[:, k, t * P:(t + 1) * P], w[:, k, :],
                                      start=(k == 0), stop=(k == KD - 1))
                        last.then_inc(o_p.sem, 1)

            def router(layer):
                w = w_slot(layer * UNITS + U_OUT + 1)[:, 4096:4608].rearrange("p (k c) -> p k c", k=KD)
                for t in range(TOUT[layer]):
                    for k in range(KD):
                        last = mm(bank[2][:, t * NE:(t + 1) * NE], hT[:, k, t * P:(t + 1) * P], w[:, k, :],
                                  start=(k == 0), stop=(k == KD - 1))
                last.then_inc(r_p.sem, 1)
                for t in range(TOUT[layer]):
                    if t >= 1:
                        pe.wait_ge(*rb_ok.at(layer, t))
                    for k in range(KD):
                        last = nc.tensor.transpose(bank[4 + k // 4][:, (k % 4) * P:(k % 4 + 1) * P],
                                                   hT[:, k, t * P:(t + 1) * P], ident)
                    last.then_inc(rb_p.sem, 1)

            def shared_expert(layer):
                n = layer * UNITS + U_SHARED
                size = TOUT[layer] * P
                w_need(n)
                w1 = w_slot(n)[:, 0:2048].rearrange("p (k c) -> p k c", k=KD)
                w3 = w_slot(n)[:, 2048:4096].rearrange("p (k c) -> p k c", k=KD)
                w2 = w_slot(n)[:, 4096:6144].rearrange("p (j d) -> p j d", j=2)
                for j in range(2):
                    if j == 1:
                        pe.wait_ge(*sh_a.at(layer, 1))
                    for i, w in enumerate((w1, w3)):
                        for k in range(KD):
                            last = mm(bank[i][:, 0:size], w[:, k, j * P:(j + 1) * P], hT[:, k, 0:size],
                                      start=(k == 0), stop=(k == KD - 1))
                    last.then_inc(sh_p.sem, 1)
                pe.wait_ge(*msk_ok.at(layer, 1))
                for t in range(TOUT[layer]):
                    for q in range(t + 1):
                        mm(bank[6][:, t * NE:(t + 1) * NE], ones if q < t else tri[0], msk[:, q, :],
                           start=(q == 0), stop=(q == t))
                for q in range(TOUT[layer]):
                    last = mm(bank[6][:, 256:256 + NE], ones, msk[:, q, :], start=(q == 0), stop=(q == TOUT[layer] - 1))
                last.then_inc(rank_p.sem, 1)
                pe.wait_ge(*sh_a.at(layer, 2))
                pe.wait_ge(*rb_ok.at(layer, TOUT[layer]))
                e = 0
                for t in range(TOUT[layer]):
                    for half in range(2):
                        e += 1
                        if e >= 3:
                            pe.wait_ge(*sh_ok.at(layer, e - 2))
                        for j in range(2):
                            last = mm(bank[4 + e % 2][:, :], a_sh[:, j, t * P:(t + 1) * P],
                                      w2[:, j, half * 512:(half + 1) * 512], start=(j == 0), stop=(j == 1))
                        last.then_inc(sh_y.sem, 1)
                pe.wait_ge(*sh_ok.at(layer, e))
                pe.wait_ge(*rank_ok.at(layer, 1))

            def table(layer, g, j):
                cap, tiles = CAPS[layer], TOUT[layer]
                for t in range(tiles):
                    last = mm(bank[6][0:cap, 0:2], sel[:, j % 2, t * cap:(t + 1) * cap], at_expert(val, t, g * 4 + j),
                              start=(t == 0), stop=(t == tiles - 1))
                return last

            def expert_in(layer, slot):
                cap = CAPS[layer]
                if cap < P:
                    pe.sem_inc(reached, 1)
                for k in range(KD):
                    last = nc.tensor.transpose(bank[k // 4][:, (k % 4) * cap:(k % 4 + 1) * cap],
                                               xg[0:cap, slot, k::KD], ident[0:cap, 0:cap])
                return last

            def expert_hidden(layer, slot, w, b):
                cap = CAPS[layer]
                w1 = w[:, 0:2048].rearrange("p (k c) -> p k c", k=KD)
                w3 = w[:, 2048:4096].rearrange("p (k c) -> p k c", k=KD)
                for i, wi in enumerate((w1, w3)):
                    for j in range(2):
                        at = (2 * i + j) * cap
                        for k in range(KD):
                            last = mm(b[:, at:at + cap], wi[:, k, j * P:(j + 1) * P],
                                      xT[:, slot, k * cap:(k + 1) * cap], start=(k == 0), stop=(k == KD - 1))
                return last

            def expert_out(layer, slot, w):
                cap = CAPS[layer]
                w2 = w[:, 4096:6144].rearrange("p (j d) -> p j d", j=2)
                for half in range(2):
                    for j in range(2):
                        last = mm(bank[4 + half][0:cap, :], act_a[:, slot, j * cap:(j + 1) * cap],
                                  w2[:, j, half * 512:(half + 1) * 512], start=(j == 0), stop=(j == 1))
                return last

            def experts(layer):
                base = layer * UNITS + U_EXP
                e0 = layer * NE

                def table_of(g, j):
                    e = g * 4 + j
                    pe.wait_ge(sel_ok.sem, e + (e0 + 1))
                    if layer or not isinstance(e, int) or e >= 1:
                        pe.wait_ge(idx_ok.sem, e + e0)
                    table(layer, g, j).then_inc(tbl_p.sem, 1)

                def transposes_of(g, j):
                    e = g * 4 + j
                    pe.wait_ge(rows_in[j % 2].sem, rows_in[j % 2].at(layer, 16)[1] + (g * 2 + j // 2) * 16)
                    if layer or not isinstance(e, int) or e >= 1:
                        pe.wait_ge(xt_v.sem, e + e0)
                        pe.wait_ge(xt_a.sem, e + e0)
                    expert_in(layer, j % 2).then_inc(xt_p.sem, 1)

                def out_of(g, j):
                    e = g * 4 + j
                    pe.wait_ge(a_ok.sem, e + (e0 + 1))
                    if layer or not isinstance(e, int) or e >= 1:
                        pe.wait_ge(y_v.sem, e + e0)
                        pe.wait_ge(y_a_ok.sem, e + e0)
                    expert_out(layer, j % 2, w_slot(base + j)).then_inc(y_p.sem, 1)

                def group(g, first=False, last=False):
                    for j in range(4):
                        e = g * 4 + j
                        n = base + j
                        pe.wait_ge(weights_in[n % WSLOTS], g * ARRIVED + ARRIVED * (n // WSLOTS + 1))
                        pe.wait_ge(xt_v.sem, e + (e0 + 1))
                        pe.wait_ge(xt_a.sem, e + (e0 + 1))
                        if layer or not first or j >= 2:
                            pe.wait_ge(a_ok.sem, e + (e0 - 1))
                        expert_hidden(layer, j % 2, w_slot(n), bank[2 + j % 2]).then_inc(h_p.sem, 1)
                        if not last or j < 3:
                            transposes_of(g, j + 1)
                        if not last or j < 2:
                            table_of(g, j + 2)
                        if not first or j >= 1:
                            out_of(g, j - 1)

                table_of(0, 0)
                table_of(0, 1)
                transposes_of(0, 0)
                group(0, first=True)
                with pe.Fori(1, NE // 4 - 1) as g:
                    group(g)
                group(NE // 4 - 1, last=True)
                out_of(NE // 4 - 1, 3)

            def further_passes(layer):
                w, used, scan, sel_s, tbl, idx, rows, xt, xte, h, sig, a, y, ye, _ = OV[layer]
                pe.sem_inc(y, 1)
                most = pe.value_load(cnt_i[0:1, :], min_val=0, max_val=NT * P)
                with pe.Fori(1, PASSES) as q:
                    with pe.If(most > q * CAPS[layer]):
                        with pe.Fori(0, NE) as e:
                            n = (q - 1) * NE + e
                            pe.wait_ge(sel_s, n + 1)
                            for t in range(TOUT[layer]):
                                cap = CAPS[layer]
                                last = mm(bank[6][0:cap, 0:2], sel[:, 0, t * cap:(t + 1) * cap], at_expert(val, t, e),
                                          start=(t == 0), stop=(t == TOUT[layer] - 1))
                            last.then_inc(tbl, 1)
                            pe.wait_ge(rows, n * 16 + 16)
                            expert_in(layer, 0).then_inc(xt, 1)
                            pe.wait_ge(xte, n * 2 + 2)
                            pe.wait_ge(w, n * ARRIVED + ARRIVED)
                            expert_hidden(layer, 0, ring[:, 0, :], bank[2]).then_inc(h, 1)
                            pe.wait_ge(a, n + 1)
                            expert_out(layer, 0, ring[:, 0, :]).then_inc(y, 1)
                            pe.wait_ge(ye, n * 2 + 2)

            for layer in range(DEPTH):
                modulation(layer)
                norm_transposes(layer, 0)
                input_projection(layer)
                pool_branch(layer)
                mlstm(layer)
                latent_attention(layer)
                merge(layer)
                output_projection(layer)
                norm_transposes(layer, 1)
                router(layer)
                shared_expert(layer)
                experts(layer)
                further_passes(layer)

        @block.vector
        def _(dve):
            v = nc.vector
            count = [0]

            def then(ins):
                count[0] += 1
                ins.then_inc(order_v, 1)
                dve.wait_ge(order_v, count[0])

            def told(ins, sig, layer, n):
                ins.then_inc(sig.sem, 1)
                dve.wait_ge(*sig.at(layer, n))

            dve.wait_ge(par_t, 2)
            v.tensor_copy(par[:, :, :], bank[6][:, 0:2 * P].rearrange("p (l n) -> p l n", l=2)[:, :, 0:ROWS]
                          ).then_inc(par_ok, 1)
            dve.wait_ge(par_ok, 1)
            dve.wait_ge(sigc_ok, 1)
            then(v.tensor_tensor(silu_c[:, 0, :], par[:, 0, R_C:R_C + 8], silu_c[:, 0, :], ALU.mult))
            v.tensor_tensor(silu_c[:, 1, :], par[:, 0, R_CCTX:R_CCTX + 8], silu_c[:, 1, :], ALU.mult
                            ).then_inc(silc_ok, 1)

            def modulation(layer):
                dve.wait_ge(*mod_p.at(layer, 8))
                then(v.tensor_tensor(mod[:, :, :], bank[7][:, 0:96].rearrange("p (c s) -> p c s", s=2),
                                     par[:, layer, R_BMOD:R_BMOD + 48].unsqueeze(2).broadcast_to([P, 48, 2]), ALU.add))
                for n, (m, g) in enumerate(((M_SC1, R_GMIX), (M_SC2, R_GFFN))):
                    ins = v.scalar_tensor_tensor(out=gain[:, n, :, :], in0=mod[:, m:m + KD, :], scalar=1.0,
                                                 in1=par[:, layer, g:g + KD].unsqueeze(2).broadcast_to([P, KD, 2]),
                                                 op0=ALU.add, op1=ALU.mult)
                told(ins, mod_ok, layer, 1)

            def norm(layer, which):
                tiles = NT if which == 0 else TOUT[layer]
                xn = xn1 if which == 0 else xn2
                shift = M_SH1 if which == 0 else M_SH2
                ss = stat[:, 0:tiles]
                for t in range(tiles):
                    ins = v.tensor_tensor_reduce(out=xn[:, t, :], in0=res[:, t, :], in1=res[:, t, :], scale=1.0,
                                                 scalar=0.0, op0=ALU.mult, op1=ALU.add, accum_out=stat[:, t:t + 1])
                told(ins, ss_ok, layer, which + 1)
                dve.wait_ge(*rt_ok.at(layer, which + 1))
                then(v.reciprocal(ss, ss))
                for t in range(tiles):
                    ins = v.tensor_scalar(xn[:, t, :], res[:, t, :], stat[:, t:t + 1], None, ALU.mult)
                told(ins, xn_ok, layer, which + 1)
                for k in range(0, KD, 2):
                    dve.wait_ge(*xn_t.at(layer, which * KD + k + 1))
                    for s in range(1 if tiles == 2 else 2):
                        ins = v.tensor_scalar(hT[:, k, s * 256:(s + 1) * 256], bank[0][:, s * 256:(s + 1) * 256],
                                              gain[:, which, k, s:s + 1], mod[:, shift + k, s:s + 1], ALU.mult, ALU.add)
                    ins.then_inc(hT_v.sem, 1)

            def input_projection(layer):
                for n in range(0, len(IN_CHUNKS), 2):
                    size = 512 if layer == 0 or IN_CHUNKS[n][2] else 256
                    dst = pT[:, n, 0:size] if n < C_CONV else cv[:, n - C_CONV, 0:size]
                    dve.wait_ge(*win_p.at(layer, n + 1))
                    if n == C_K:
                        ins = v.tensor_scalar(dst, bank[n % 4][:, 0:size], DH ** -0.5, None, ALU.mult)
                    else:
                        ins = v.tensor_copy(dst, bank[n % 4][:, 0:size])
                    ins.then_inc(win_v.sem, 1)
                dve.wait_ge(*win_v.at(layer, 10))
                dve.wait_ge(*win_a_ok.at(layer, 9))

            def gate_values(layer):
                dve.wait_ge(*gk_p.at(layer, 1))
                dve.wait_ge(*in_row.at(layer, 64))
                for s, d in gate_steps(layer):
                    t = ORDER[d][s]
                    v.tensor_tensor(lg[:, s, d, :, :].rearrange("p i h -> p (i h)"),
                                    bank[4][:, t * 64 + 8 * d:t * 64 + 8 * d + 8], b_gatebias[:, 8 * d:8 * d + 8], ALU.add)
                then(v.tensor_copy(krt, bank[4][:, 0:256].rearrange("p (t n) -> p t n", t=4)[:, :, 16:16 + ROPE]))
                f = lg[:, :, :, 1, :]
                told(v.scalar_tensor_tensor(out=t_a.rearrange("p s (d h) -> p s d h", d=2), in0=f, scalar=-1.0, in1=f,
                                            op0=ALU.mult, op1=ALU.max), lg_ok, layer, 1)
                dve.wait_ge(*elf_ok.at(layer, 1))
                told(v.scalar_tensor_tensor(out=lfm, in0=f, scalar=0.0, in1=ebias.rearrange("p s (d h) -> p s d h", d=2),
                                            op0=ALU.min, op1=ALU.subtract), lf_ok, layer, 1)

            def conv_branch(layer):
                n = len(row_groups(layer))
                size = n * 256
                then(v.memset(pad_z, 0.0))
                for c in range(2):
                    def rows(i):
                        return cv[:, i + c, 0:size].rearrange("p (s t) -> p s t", s=n)
                    acc = acc_c[:, 0:size].rearrange("p (s t) -> p s t", s=n)
                    then(v.tensor_tensor(pad_z[:, 0:n, 1:257], rows(4), rows(0), ALU.mult))
                    wcol = [par[:, layer, R_CONVW + 2 * j + c:R_CONVW + 2 * j + c + 1] for j in range(3)]
                    then(v.tensor_scalar(acc, pad_z[:, 0:n, 0:256], wcol[0],
                                         par[:, layer, R_CONVB + c:R_CONVB + c + 1], ALU.mult, ALU.add))
                    for j in (1, 2):
                        then(v.scalar_tensor_tensor(out=acc, in0=pad_z[:, 0:n, j:j + 256], scalar=wcol[j], in1=acc,
                                                    op0=ALU.mult, op1=ALU.add))
                    ins = v.tensor_tensor(Y[:, 6 + c, 0:size].rearrange("p (s t) -> p s t", s=n), acc, rows(2), ALU.mult)
                    if c == 0:
                        then(ins)
                told(ins, conv_ok, layer, 1)

            def pool_branch(layer):
                n = len(row_groups(layer))
                size = n * 256
                dve.wait_ge(*in_cnt.at(layer, 16))
                then(v.memset(pad_u, 0.0))
                for c in range(2):
                    u = pT[:, C_POOL + c, 0:size].rearrange("p (s t) -> p s t", s=n)
                    then(v.tensor_copy(pad_u[:, 0:n, 8:264], u))
                    then(v.tensor_tensor(win_a[:, 0:n, 1:272], pad_u[:, 0:n, 0:271], pad_u[:, 0:n, 1:272], ALU.add))
                    then(v.tensor_tensor(win_b[:, 0:n, 2:271], win_a[:, 0:n, 1:270], win_a[:, 0:n, 3:272], ALU.add))
                    if c == 1:
                        then(v.tensor_tensor(win_a[:, 0:n, 4:269], win_b[:, 0:n, 2:267], win_b[:, 0:n, 6:271], ALU.add))
                        then(v.tensor_tensor(win_b[:, 0:n, 8:264], win_a[:, 0:n, 4:260], win_a[:, 0:n, 12:268], ALU.add))
                    for a, win in enumerate((win_a, win_b)):
                        q = slice(a * 64, a * 64 + 64)
                        cnt = inv_cnt[q, c, :].unsqueeze(1).broadcast_to([64, n, 256])
                        then(v.tensor_tensor(win[q, 0:n, 8:264], win[q, 0:n, 8:264], cnt, ALU.mult))
                        ins = v.tensor_tensor(u[q], win[q, 0:n, 8:264], u[q], ALU.subtract)
                        if (c, a) != (1, 1):
                            then(ins)
                told(ins, pool_in, layer, 1)

            def mlstm(layer):
                then(v.memset(vaug[:, :, :, 64:65], 1.0))
                for t in range(NT):
                    dve.wait_ge(*kv_p.at(layer, t + 1))
                    b = bank[5 + t % 2]
                    v.tensor_copy(ktok[:, t, :], b[:, 0:256])
                    v.tensor_copy(vaug[:, t, :, 0:64], b[:, 256:512].rearrange("p (h e) -> p h e", h=4)
                                  ).then_inc(kv_ok.sem, 1)
                dve.wait_ge(*kv_ok.at(layer, 4))
                dve.wait_ge(*b_p.at(layer, 1))
                then(v.tensor_copy(sm[:, 96:160], bank[4][:, 0:64]))
                then(v.tensor_tensor(uu.rearrange("p s (d h) -> p s d h", d=2), lg[:, :, :, 0, :],
                                     cumf.rearrange("p s (d h) -> p s d h", d=2), ALU.subtract))
                then(v.memset(cmax, 0.0))
                dve.wait_ge(*pool_p.at(layer, 2))
                for n, (s, d) in enumerate(gate_steps(layer)):
                    if n >= 1:
                        dve.wait_ge(*ub_p.at(layer, n))
                    u4 = uu[:, s, 4 * d:4 * d + 4]
                    v.tensor_tensor(dg.rearrange("p (h t) -> p h t", h=4), ident.unsqueeze(1).broadcast_to([P, 4, P]),
                                    u4.unsqueeze(2).broadcast_to([P, 4, P]), ALU.mult).then_inc(dg_ok.sem, 1)
                    dve.wait_ge(*ub_p.at(layer, n + 1))
                    ub = bank[n % 2][:, :].rearrange("p (h t) -> p h t", h=4)
                    ins = v.tensor_reduce(umax[:, s, 4 * d:4 * d + 4], ub, AX.X, ALU.max)
                    if emits(layer, s):
                        then(v.tensor_tensor(dm[:, n], ub, mask[d].unsqueeze(1).broadcast_to([P, 4, P]), ALU.add))
                        ins = v.tensor_reduce(cmax[:, s, 4 * d:4 * d + 4], dm[:, n], AX.X, ALU.max)
                    told(ins, ub_used, layer, n + 1)
                then(v.tensor_tensor(umax, endf, umax, ALU.add))
                then(v.memset(m_st[:, 0, :], 0.0))
                for s in range(4):
                    then(v.tensor_tensor(t_a[:, s, :], endf[:, s, :], m_st[:, s, :], ALU.add))
                    then(v.tensor_tensor(m_st[:, s + 1, :], t_a[:, s, :], umax[:, s, :], ALU.max))
                then(v.tensor_tensor(a_int, cumf, m_st[:, 0:4, :], ALU.add))
                then(v.tensor_tensor(cmax, cumf, cmax, ALU.add))
                then(v.tensor_tensor(emt, a_int, cmax, ALU.max))
                then(v.tensor_tensor(a_int, a_int, emt, ALU.subtract))
                then(v.tensor_tensor(ebias, cumf, emt, ALU.subtract))
                then(v.tensor_tensor(decay, t_a, m_st[:, 1:5, :], ALU.subtract))
                then(v.tensor_tensor(w_s, endf, uu, ALU.add))
                told(v.tensor_tensor(w_s, w_s, m_st[:, 1:5, :], ALU.subtract), mg_ok, layer, 1)
                dve.wait_ge(*mx_ok.at(layer, 1))
                e = st = 0
                seen = set()
                for n, (s, d) in enumerate(gate_steps(layer)):
                    t = ORDER[d][s]
                    col = slice(4 * d, 4 * d + 4)
                    if emits(layer, s):
                        e += 1
                        dve.wait_ge(*w_ok.at(layer, e))
                        dve.wait_ge(*s_p.at(layer, e))
                        if e >= 2:
                            dve.wait_ge(*pt_p.at(layer, e - 1))
                        for a in range(2):
                            ins = v.tensor_tensor(pm[:, a::2, :], bank[a][:, 0:256].rearrange("p (h t) -> p h t", h=2),
                                                  dm[:, n, a::2, :], ALU.mult)
                        ins.then_inc(p_ok.sem, 1)
                    if s < 3:
                        st += 1
                        if st >= 2:
                            dve.wait_ge(*st_p.at(layer, st - 1))
                        v.tensor_tensor(kw.rearrange("p (h e) -> p h e", h=4), ktok[:, t, :].rearrange("p (h e) -> p h e", h=4),
                                        w_s[:, s, col].unsqueeze(2).broadcast_to([P, 4, 64]), ALU.mult
                                        ).then_inc(kw_ok.sem, 1)
                    if emits(layer, s):
                        dve.wait_ge(*av_p.at(layer, e))
                        av = bank[3][:, 0:260].rearrange("p (h e) -> p h e", h=4)
                        if s > 0:
                            for a in range(2):
                                then(v.tensor_tensor(num[:, a::2, :], bank[4 + a][:, 0:130].rearrange("p (h e) -> p h e", h=2),
                                                     a_int[:, s, 4 * d + a:4 * d + 4:2].unsqueeze(2).broadcast_to([P, 2, 65]),
                                                     ALU.mult))
                            told(v.tensor_tensor(num, av, num, ALU.add), av_used, layer, e)
                        else:
                            told(v.tensor_copy(num, av), av_used, layer, e)
                        then(v.scalar_tensor_tensor(out=den, in0=num[:, :, 64], scalar=-1.0, in1=num[:, :, 64],
                                                    op0=ALU.mult, op1=ALU.max))
                        then(v.tensor_tensor(den, den, emt[:, s, col], ALU.max))
                        then(v.reciprocal(den, den))
                        rec = den.unsqueeze(2).broadcast_to([P, 4, 64])
                        if t in seen:
                            then(v.tensor_tensor(hd, num[:, :, 0:64], rec, ALU.mult))
                            then(v.tensor_tensor(hsum[:, t], hsum[:, t], hd, ALU.add))
                        else:
                            then(v.tensor_tensor(hsum[:, t], num[:, :, 0:64], rec, ALU.mult))
                        seen.add(t)
                    if s < 3:
                        dve.wait_ge(*st_p.at(layer, st))
                        for h in range(HEADS):
                            q = slice((h % 2) * 64, (h % 2) * 64 + 64)
                            new = bank[6][q, (h // 2) * 130 + (h % 2) * 65:(h // 2) * 130 + (h % 2) * 65 + 65]
                            if s == 0:
                                ins = v.tensor_copy(cstate[q, d, h // 2, :], new)
                            else:
                                ins = v.scalar_tensor_tensor(out=cstate[q, d, h // 2, :], in0=cstate[q, d, h // 2, :],
                                                             scalar=decay[q, s, 4 * d + h:4 * d + h + 1], in1=new,
                                                             op0=ALU.mult, op1=ALU.add)
                        told(ins, c_ok, layer, st)
                tiles = TOUT[layer]
                then(v.tensor_tensor(hsq[:, 0:tiles], hsum[:, 0:tiles], hsum[:, 0:tiles], ALU.mult))
                told(v.tensor_reduce(hss[:, 0:tiles, :], hsq[:, 0:tiles], AX.X, ALU.add), hss_ok, layer, 1)
                dve.wait_ge(*hrt_ok.at(layer, 1))
                then(v.reciprocal(hss[:, 0:tiles, :], hss[:, 0:tiles, :]))
                ht = hsum[:, 0:tiles].rearrange("p t h e -> p (t h) e")
                told(v.tensor_tensor(ht, ht, Y[:, 1, 272:272 + 4 * tiles].unsqueeze(2).broadcast_to([P, 4 * tiles, 64]), ALU.mult),
                     hn_ok, layer, 1)
                dve.wait_ge(*sigo_ok.at(layer, 1))
                for t in range(tiles):
                    dve.wait_ge(*hn_p.at(layer, t + 1))
                    tok = slice(t * P, (t + 1) * P)
                    for c in range(2):
                        ins = v.scalar_tensor_tensor(out=Y[:, c, tok], in0=bank[t % 2][:, c * P:(c + 1) * P],
                                                     scalar=par[:, layer, R_HGAIN + c:R_HGAIN + c + 1],
                                                     in1=pT[:, C_O + c, tok], op0=ALU.mult, op1=ALU.mult)
                    ins.then_inc(yml_ok.sem, 1)
                dve.wait_ge(*yml_ok.at(layer, tiles))

            def latent_attention(layer):
                tiles = TOUT[layer]
                size = tiles * P
                v.tensor_tensor(sq_c[:, :, 0:size], pT[:, C_CQ:C_CQ + 2, 0:size], pT[:, C_CQ:C_CQ + 2, 0:size], ALU.mult)
                then(v.tensor_tensor(sq_kv, pT[:, C_CKV, :], pT[:, C_CKV, :], ALU.mult))
                for c in range(2):
                    v.tensor_scalar(pT[:, C_CQ + c, 0:size], pT[:, C_CQ + c, 0:size],
                                    par[:, layer, R_GCQ + c:R_GCQ + c + 1], None, ALU.mult)
                told(v.tensor_scalar(pT[:, C_CKV, :], pT[:, C_CKV, :], par[:, layer, R_GCKV:R_GCKV + 1], None, ALU.mult),
                     sqc_ok, layer, 1)
                dve.wait_ge(*rtc_ok.at(layer, 1))
                st2 = stat[:, 0:8].rearrange("p (t i) -> p t i", i=2)
                then(v.reciprocal(st2[:, 0:tiles, 0], st2[:, 0:tiles, 0]))
                told(v.reciprocal(st2[:, :, 1], st2[:, :, 1]), rsc_ok, layer, 1)
                for t in range(NT):
                    n0 = 0 if t < tiles else 1
                    m = (2 - n0) * 4
                    x = qk_t[:, n0:2].rearrange("p n h e -> p (n h) e")
                    x2 = qk_s[:, n0:2].rearrange("p n h e -> p (n h) e")
                    ss = stat[:, 8 + 4 * n0:16]
                    dve.wait_ge(*qk_ok.at(layer, t + 1))
                    then(v.tensor_copy(qk_t[:, 1, :, NOPE:QK], krt[:, t, :].unsqueeze(1).broadcast_to([P, 4, ROPE])))
                    then(v.tensor_tensor(x2, x, x, ALU.mult))
                    told(v.tensor_reduce(ss, x2, AX.X, ALU.add), qss_ok, layer, t + 1)
                    dve.wait_ge(*qrt_ok.at(layer, t + 1))
                    then(v.reciprocal(ss, ss))
                    then(v.tensor_tensor(x, x, ss.unsqueeze(2).broadcast_to([P, m, QK]), ALU.mult))
                    for n in range(n0, 2):
                        ins = v.tensor_tensor(qk_t[:, n], qk_t[:, n],
                                              (b_gqn, b_gkn)[n].unsqueeze(1).broadcast_to([P, 4, QK]), ALU.mult)
                        if n == 0 or t < 2:
                            then(ins)
                    if t < 2:
                        r = x[:, :, NOPE:QK]
                        t1 = x2[:, :, 0:ROPE]
                        t2 = qk_r[:, n0:2].rearrange("p n h e -> p (n h) e")
                        cosr = cst[:, K_RC + 32 * t:K_RC + 32 * t + 32].unsqueeze(1).broadcast_to([P, m, 32])
                        v.tensor_tensor(t1, r, cosr, ALU.mult)
                        for half in range(2):
                            for pair in range(2):
                                a, b = half * 16 + pair * 8, half * 16 + (1 - pair) * 8
                                sinr = cst[:, K_RS + 32 * t + a:K_RS + 32 * t + a + 8].unsqueeze(1).broadcast_to([P, m, 8])
                                ins = v.tensor_tensor(t2[:, :, a:a + 8], r[:, :, b:b + 8], sinr, ALU.mult)
                        then(ins)
                        ins = v.tensor_tensor(r, t1, t2, ALU.add)
                    told(ins, qkn_ok, layer, t + 1)
                    dve.wait_ge(*qkt_p.at(layer, t + 1))
                    v.tensor_copy(kT_a[0:QK, :, t * P:(t + 1) * P], bank[3][0:QK, :].rearrange("p (h t) -> p h t", h=4)
                                  ).then_inc(kT_ok.sem, 1)
                pairs = [(t, h) for t in range(tiles) for h in range(HEADS)]

                def turned(n):
                    t, h = pairs[n]
                    size = 512 if t < 2 else 256
                    dve.wait_ge(*at_p.at(layer, n + 1))
                    if n >= 2:
                        dve.wait_ge(*aav_p.at(layer, n - 1))
                    v.tensor_copy(paT[:, n % 2, 0:size], bank[2 + n % 2][:, 0:size]).then_inc(at_ok.sem, 1)
                    if h == HEADS - 1:
                        dve.wait_ge(*aav_p.at(layer, n + 1))
                        rs = asum[:, t % 2, :]
                        then(v.reciprocal(rs, rs))
                        if t >= 1:
                            dve.wait_ge(*ya_p.at(layer, t))
                        v.tensor_tensor(y_a.rearrange("p (h e) -> p h e", h=4), bank[7][:, 0:256].rearrange("p (h e) -> p h e", h=4),
                                        rs.unsqueeze(2).broadcast_to([P, 4, 64]), ALU.mult).then_inc(ya_ok.sem, 1)

                for n in range(len(pairs) + 1):
                    if n < len(pairs):
                        size = 512 if pairs[n][0] < 2 else 256
                        dve.wait_ge(*as_p.at(layer, n + 1))
                        if n >= 2:
                            dve.wait_ge(*ae_ok.at(layer, n - 1))
                        mx = stat[:, 16 + n % 2:17 + n % 2]
                        then(v.tensor_reduce(mx, bank[5 + n % 2][:, 0:size], AX.X, ALU.max, negate=True))
                        v.tensor_scalar(mx, mx, QK ** -0.5, None, ALU.mult).then_inc(am_ok.sem, 1)
                    if n >= 1:
                        turned(n - 1)

            def merge(layer):
                size = TOUT[layer] * P
                dve.wait_ge(*ya_p.at(layer, TOUT[layer]))
                told(v.memset(accT, 0.0), macc_ok, layer, 1)
                with dve.Fori(0, 2) as i:
                    for at in range(16):
                        k, slot = (at // 4 % 2) * 4 + at % 4, at % 2
                        now = i * 16 + (32 * layer + at + 1)
                        dve.wait_ge(mgate_a.sem, now)
                        dve.wait_ge(mbr_p.sem, now)
                        sg = sg_m[:, slot, 0:size]
                        v.tensor_tensor(sg, bank[2 + slot][:, 0:size], sg, ALU.mult).then_inc(mprod_ok.sem, 1)
                        dve.wait_ge(mprod_ok.sem, now)
                        v.tensor_tensor(accT[:, k, 0:size], accT[:, k, 0:size], sg, ALU.add).then_inc(macc_ok.sem, 1)
                        dve.wait_ge(macc_ok.sem, now + (layer + 1))

            def output_projection(layer):
                groups = len(row_groups(layer))
                n = 0
                for g, m in enumerate((M_GT1, M_GT2)):
                    for s in range(groups):
                        for half in range(2):
                            if n >= 1:
                                dve.wait_ge(*gb_p.at(layer, n))
                            n += 1
                            col = mod[:, m + 4 * half:m + 4 * half + 4, s:s + 1]
                            v.tensor_tensor(dgm.rearrange("p (k t) -> p k t", k=4), ident.unsqueeze(1).broadcast_to([P, 4, P]),
                                            col.broadcast_to([P, 4, P]), ALU.mult).then_inc(gdg_ok.sem, 1)
                dve.wait_ge(*gb_ok.at(layer, n))
                e = 0
                for half in range(2):
                    for t in range(TOUT[layer]):
                        e += 1
                        dve.wait_ge(*o_p.at(layer, e))
                        add_gated(bank[e % 2], 0, t, half, o_ok, layer, e)

            def add_gated(b, g, t, half, sig, layer, n):
                cols = slice(half * 512, half * 512 + 512)
                told(v.tensor_tensor(upd[:, 0, :], b[:, :], gt_b[:, g, t // 2, cols], ALU.mult), sig, layer, n)
                then(v.tensor_tensor(res[:, t, cols], res[:, t, cols], upd[:, 0, :], ALU.add))

            def route_tile(layer, t):
                iota64 = cst[:, K_IOTA:K_IOTA + NE]
                then(v.tensor_tensor(sb_r, sc_r[:, t, :], b_router, ALU.add))
                then(v.max(mx8, sb_r))
                then(v.max_index(ix8, mx8, sb_r))
                then(v.tensor_copy(ixf, ix8))
                then(v.tensor_tensor(oh, iota64.unsqueeze(1).broadcast_to([P, TOPK, NE]),
                                     ixf[:, 0:TOPK].unsqueeze(2).broadcast_to([P, TOPK, NE]), ALU.is_equal))
                then(v.tensor_reduce(msk[:, t, :], oh.rearrange("p j e -> p e j"), AX.X, ALU.add))
                then(v.tensor_tensor(oh2, oh, cst[:, K_IOTA:K_IOTA + TOPK].unsqueeze(2).broadcast_to([P, TOPK, NE]), ALU.mult))
                then(v.tensor_reduce(vj, oh2.rearrange("p j e -> p e j"), AX.X, ALU.add))
                then(v.scalar_tensor_tensor(out=val[:, t, :, 0], in0=msk[:, t, :], scalar=tok6[:, t:t + 1], in1=vj,
                                            op0=ALU.mult, op1=ALU.add))
                then(v.tensor_copy(val[:, t, :, 1], cst[:, K_TOK + t:K_TOK + t + 1].broadcast_to([P, NE])))
                then(v.tensor_tensor(oh2, oh, sc_r[:, t, :].unsqueeze(1).broadcast_to([P, TOPK, NE]), ALU.mult))
                w = wgt[:, t, 0:TOPK]
                then(v.tensor_reduce(w, oh2, AX.X, ALU.add))
                then(v.tensor_reduce(sumw[:, 0:1], w, AX.X, ALU.add))
                then(v.reciprocal(sumw[:, 1:2], sumw[:, 0:1]))
                then(v.tensor_scalar(w, w, sumw[:, 1:2], ROUTE_SCALE, ALU.mult, ALU.mult))

            def router_and_shared_expert(layer):
                tiles = TOUT[layer]
                size = tiles * P
                then(v.tensor_scalar(tok6, cst[:, K_TOK:K_TOK + 4], float(TOPK), 1.0, ALU.mult, ALU.add))
                dve.wait_ge(*r_sc.at(layer, 1))
                for j in range(2):
                    dve.wait_ge(*sh_sig.at(layer, j + 1))
                    then(v.tensor_tensor(sg_sh[:, j, 0:size], bank[0][:, 0:size], sg_sh[:, j, 0:size], ALU.mult))
                    told(v.tensor_tensor(a_sh[:, j, 0:size], bank[1][:, 0:size], sg_sh[:, j, 0:size], ALU.mult),
                         sh_a, layer, j + 1)
                    for t in range(tiles // 2 * j, tiles // 2 * (j + 1)):
                        route_tile(layer, t)
                v.memset(cnt_f, 0.0).then_inc(msk_ok.sem, 1)
                dve.wait_ge(*rank_p.at(layer, 1))
                dve.wait_ge(*msk_ok.at(layer, 1))
                rk = rank[:, 0:tiles, :]
                then(v.tensor_tensor(rk, bank[6][:, 0:tiles * NE].rearrange("p (t e) -> p t e", t=tiles),
                                     msk[:, 0:tiles, :], ALU.mult))
                then(v.tensor_scalar(rk, rk, -1.0, None, ALU.add))
                then(v.tensor_reduce(cnt_f, bank[6][:, 256:256 + NE], AX.X, ALU.max))
                told(v.tensor_copy(cnt_i, cnt_f), rank_ok, layer, 1)
                e = 0
                for t in range(tiles):
                    for half in range(2):
                        e += 1
                        dve.wait_ge(*sh_y.at(layer, e))
                        add_gated(bank[4 + e % 2], 1, t, half, sh_ok, layer, e)

            def select(layer, slot, e):
                cap = CAPS[layer]
                for t in range(TOUT[layer]):
                    col = rank[:, t, e:e + 1] if isinstance(e, int) else rank[:, t, bass.ds(e, 1)]
                    last = v.tensor_scalar(sel[:, slot, t * cap:(t + 1) * cap], cst[:, K_IOTA:K_IOTA + cap], col, None,
                                           ALU.is_equal)
                return last

            def row_indices(layer, i, mark, now):
                cap = CAPS[layer]
                v.tensor_scalar(tmp1[0:cap], bank[6][0:cap, 0:1], 0.0, BIG, ALU.is_equal, ALU.mult).then_inc(mark, 1)
                dve.wait_ge(mark, now)
                v.tensor_copy(idx_g[i][0:cap], bank[6][0:cap, 1:2])
                return v.scalar_tensor_tensor(out=idx_s[i][0:cap], in0=bank[6][0:cap, 0:1], scalar=-1.0,
                                              in1=tmp1[0:cap], op0=ALU.add, op1=ALU.add)

            def gated_hidden(layer, slot, b, mark, now):
                cap = CAPS[layer]
                sg = sig_a[:, slot, 0:2 * cap]
                v.tensor_tensor(sg, b[:, 0:2 * cap], sg, ALU.mult).then_inc(mark, 1)
                dve.wait_ge(mark, now)
                return v.tensor_tensor(act_a[:, slot, 0:2 * cap], b[:, 2 * cap:4 * cap], sg, ALU.mult)

            def experts(layer):
                cap = CAPS[layer]
                e0 = layer * NE

                def select_of(g, j):
                    e = g * 4 + j
                    if layer or not isinstance(e, int) or e >= 2:
                        dve.wait_ge(tbl_p.sem, e + (e0 - 1))
                    select(layer, j % 2, e).then_inc(sel_ok.sem, 1)

                def indices_of(g, j):
                    now = g * 4 + (j + e0 + 1)
                    dve.wait_ge(tbl_p.sem, now)
                    if not isinstance(g, int) or g * 4 + j >= 4:
                        dve.wait_ge(y_out.sem, (g * 4 + j - 3) * 16 + 16 * e0)
                    row_indices(layer, j % 4, empty_ok.sem, now).then_inc(idx_ok.sem, 1)
                    dve.wait_ge(idx_ok.sem, now)

                def input_of(g, j):
                    dve.wait_ge(xt_p.sem, g * 4 + (j + e0 + 1))
                    v.tensor_copy(xT[:, j % 2, 0:4 * cap], bank[0][:, 0:4 * cap]).then_inc(xt_v.sem, 1)

                def hidden_of(g, j):
                    now = g * 4 + (j + e0 + 1)
                    dve.wait_ge(h_sig.sem, now)
                    gated_hidden(layer, j % 2, bank[2 + j % 2], hprod_ok.sem, now).then_inc(a_ok.sem, 1)

                def output_of(g, j):
                    e = g * 4 + j
                    dve.wait_ge(y_p.sem, e + (e0 + 1))
                    if layer or not isinstance(e, int) or e >= 1:
                        dve.wait_ge(y_out.sem, e * 16 + 16 * e0)
                    v.tensor_copy(ysb[0:cap, 0:512], bank[4][0:cap, :]).then_inc(y_v.sem, 1)

                def group(g, first=False, last=False):
                    for j in range(4):
                        if not last or j < 2:
                            select_of(g, j + 2)
                        if not last or j < 3:
                            input_of(g, j + 1)
                        hidden_of(g, j)
                        if not last or j < 2:
                            indices_of(g, j + 2)
                        if not first or j >= 1:
                            output_of(g, j - 1)

                select_of(0, 0)
                select_of(0, 1)
                indices_of(0, 0)
                indices_of(0, 1)
                input_of(0, 0)
                group(0, first=True)
                with dve.Fori(1, NE // 4 - 1) as g:
                    group(g)
                group(NE // 4 - 1, last=True)
                output_of(NE // 4 - 1, 3)

            def further_passes(layer):
                cap = CAPS[layer]
                w, used, scan, sel_s, tbl, idx, rows, xt, xte, h, sig, a, y, ye, sent = OV[layer]
                most = dve.value_load(cnt_i[0:1, :], min_val=0, max_val=NT * P)
                with dve.Fori(1, PASSES) as q:
                    with dve.If(most > q * cap):
                        rk = rank[:, 0:TOUT[layer], :]
                        dve.wait_ge(*y_v.at(layer, NE))
                        v.tensor_scalar(rk, rk, -float(cap), None, ALU.add).then_inc(scan, 1)
                        dve.wait_ge(scan, q)
                        dve.sem_inc(reached, 1)
                        with dve.Fori(0, NE) as e:
                            n = (q - 1) * NE + e
                            select(layer, 0, e).then_inc(sel_s, 1)
                            dve.wait_ge(tbl, n + 1)
                            row_indices(layer, 0, used, n * 2 + 1).then_inc(idx, 1)
                            dve.wait_ge(xt, n + 1)
                            v.tensor_copy(xT[:, 0, 0:4 * cap], bank[0][:, 0:4 * cap]).then_inc(xte, 1)
                            dve.wait_ge(sig, n + 1)
                            gated_hidden(layer, 0, bank[2], used, n * 2 + 2).then_inc(a, 1)
                            dve.wait_ge(y, n + 2)
                            v.tensor_copy(ysb[0:cap, 0:512], bank[4][0:cap, :]).then_inc(ye, 1)
                            dve.wait_ge(sent, n * 16 + 16)

            def combine(layer):
                n = 0
                for t in range(TOUT[layer]):
                    for half in range(2):
                        cols = slice(half * 512, half * 512 + 512)
                        rows = comb[:, n % 2]
                        dve.wait_ge(*comb_in[n % 2].at(layer, 16 * (n // 2 + 1)))
                        then(v.tensor_scalar(cacc, rows[:, 0, :], wgt[:, t, 0:1], None, ALU.mult))
                        for j in range(1, TOPK):
                            ins = v.scalar_tensor_tensor(out=cacc, in0=rows[:, j, :], scalar=wgt[:, t, j:j + 1], in1=cacc,
                                                         op0=ALU.mult, op1=ALU.add)
                            if j < TOPK - 1:
                                then(ins)
                        n += 1
                        told(ins, comb_used, layer, n)
                        then(v.tensor_tensor(cacc, cacc, gt_b[:, 1, t // 2, cols], ALU.mult))
                        then(v.tensor_tensor(res[:, t, cols], res[:, t, cols], cacc, ALU.add))
                v.memset(tmp1, 0.0).then_inc(res_ok, 1)
                dve.wait_ge(res_ok, layer + 1)

            dve.wait_ge(in_res, 32)
            for layer in range(DEPTH):
                modulation(layer)
                norm(layer, 0)
                input_projection(layer)
                gate_values(layer)
                conv_branch(layer)
                pool_branch(layer)
                mlstm(layer)
                latent_attention(layer)
                merge(layer)
                output_projection(layer)
                norm(layer, 1)
                router_and_shared_expert(layer)
                experts(layer)
                further_passes(layer)
                combine(layer)

        @block.scalar
        def _(act):
            fn = nc.scalar.activation

            act.dma_start(cst[:, :], consts).then_inc(in_const, 16)
            for layer in range(DEPTH):
                rows_of = ((R_BMOD, 48, b_mod[layer]), (R_GMIX, 8, g_mix[layer]), (R_GFFN, 8, g_ffn[layer]),
                           (R_BGATE, 32, b_gate[layer].rearrange("i d -> (i d)")), (R_HGAIN, 2, ml_head_gain[layer]),
                           (R_PSCALE, 2, pool_scale[layer]), (R_CONVW, 6, conv_w[layer].rearrange("j d -> (j d)")),
                           (R_CONVB, 2, conv_b[layer]), (R_GCQ, 2, mla_g_cq[layer]), (R_GCKV, 1, mla_g_ckv[layer]),
                           (R_C, 8, c[0]), (R_CCTX, 8, c_ctx))
                for at, n, src in rows_of:
                    act.dma_start(par_raw[at:at + n, layer, :], src.rearrange("(n p) -> n p", p=P)).then_inc(in_par, 16)
            act.dma_start(res[:, 0:2, :], x[0].rearrange("(t p) d -> p t d", p=P)).then_inc(in_res, 16)
            act.dma_start(res[:, 2:4, :], ctx_in[0].rearrange("(t p) d -> p t d", p=P)).then_inc(in_res, 16)
            act.wait_ge(par_ok, 1)
            fn(silu_c[:, :, :].rearrange("p s k -> p (s k)"), par[:, 0, R_C:R_C + 16], ACT.Sigmoid).then_inc(sigc_ok, 1)

            def norm(layer, which):
                tiles = NT if which == 0 else TOUT[layer]
                shift = M_SH1 if which == 0 else M_SH2
                act.wait_ge(*ss_ok.at(layer, which + 1))
                fn(stat[:, 0:tiles], stat[:, 0:tiles], ACT.Sqrt, bias=eps, scale=1.0 / D).then_inc(rt_ok.sem, 1)
                for k in range(1, KD, 2):
                    act.wait_ge(*xn_t.at(layer, which * KD + k + 1))
                    for s in range(1 if tiles == 2 else 2):
                        ins = fn(hT[:, k, s * 256:(s + 1) * 256], bank[1][:, s * 256:(s + 1) * 256], ACT.Identity,
                                 bias=mod[:, shift + k, s:s + 1], scale=gain[:, which, k, s:s + 1])
                    ins.then_inc(hT_a.sem, 1)

            def input_projection(layer):
                for n in range(1, len(IN_CHUNKS), 2):
                    size = 512 if layer == 0 or IN_CHUNKS[n][2] else 256
                    dst = pT[:, n, 0:size] if n < C_CONV else cv[:, n - C_CONV, 0:size]
                    act.wait_ge(*win_p.at(layer, n + 1))
                    fn(dst, bank[n % 4][:, 0:size], ACT.Copy, scale=DH ** -0.5 if n == C_K + 1 else 1.0
                       ).then_inc(win_a_ok.sem, 1)

            def gates(layer):
                act.wait_ge(*lg_ok.at(layer, 1))
                fn(ebias, t_a, ACT.Exp, scale=-1.0).then_inc(order_a, 1)
                act.wait_ge(order_a, layer + 1)
                fn(ebias, ebias, ACT.Ln, bias=cst[:, K_ONE:K_ONE + 1]).then_inc(elf_ok.sem, 1)

            def pool_branch(layer):
                size = TOUT[layer] * P
                for c in range(2):
                    act.wait_ge(*pool_p.at(layer, c + 1))
                    for a in range(2):
                        q = slice(a * 64, a * 64 + 64)
                        ins = fn(Y[q, 4 + c, 0:size], bank[a][q, 0:size], ACT.Copy,
                                 scale=par[q, layer, R_PSCALE + c:R_PSCALE + c + 1])
                    ins.then_inc(pool_y.sem, 1)

            def mlstm(layer):
                act.wait_ge(*mg_ok.at(layer, 1))
                fn(emt, emt, ACT.Exp, scale=-1.0)
                exps = sm[:, 96 + 32 * 8:96 + 32 * 11]
                fn(exps, exps, ACT.Exp).then_inc(mx_ok.sem, 1)
                e = 0
                todo = []
                for n, (s, d) in enumerate(gate_steps(layer)):
                    if emits(layer, s):
                        todo.append((n, s, d))

                def weights_of(n, s, d):
                    for h in range(HEADS):
                        ins = fn(dm[:, n, h, :], dm[:, n, h, :], ACT.Exp, bias=ebias[:, s, 4 * d + h:4 * d + h + 1])
                    ins.then_inc(w_ok.sem, 1)

                weights_of(*todo[0])
                for e in range(len(todo)):
                    if e + 1 < len(todo):
                        weights_of(*todo[e + 1])
                    act.wait_ge(*pt_p.at(layer, e + 1))
                    if e >= 1:
                        act.wait_ge(*av_p.at(layer, e))
                    fn(ptm, bank[2][:, :].rearrange("p (h t) -> p h t", h=4), ACT.Copy).then_inc(pt_ok.sem, 1)
                tiles = TOUT[layer]
                act.wait_ge(*hss_ok.at(layer, 1))
                fn(hss[:, 0:tiles, :], hss[:, 0:tiles, :], ACT.Sqrt, bias=eps, scale=1.0 / DH).then_inc(hrt_ok.sem, 1)
                act.wait_ge(*win_v.at(layer, 10))
                act.wait_ge(*win_a_ok.at(layer, 9))
                size = tiles * P
                fn(pT[:, C_O:C_O + 2, 0:size], pT[:, C_O:C_O + 2, 0:size], ACT.Sigmoid).then_inc(sigo_ok.sem, 1)

            def latent_attention(layer):
                tiles = TOUT[layer]
                act.wait_ge(*ssc_p.at(layer, 1))
                st2 = stat[:, 0:8].rearrange("p (t i) -> p t i", i=2)
                ps2 = bank[4][:, 0:8].rearrange("p (t i) -> p t i", i=2)
                fn(st2[:, 0:tiles, 0], ps2[:, 0:tiles, 0], ACT.Sqrt, bias=eps, scale=1.0 / 256)
                fn(st2[:, :, 1], ps2[:, :, 1], ACT.Sqrt, bias=eps, scale=1.0 / 128).then_inc(rtc_ok.sem, 1)
                act.wait_ge(*rsc_ok.at(layer, 1))
                for t in range(NT):
                    n0 = 0 if t < tiles else 1
                    act.wait_ge(*qk_p.at(layer, t + 1))
                    if t >= 1:
                        act.wait_ge(*qkt_p.at(layer, t))
                    if t < tiles:
                        fn(qk_t[:, 0], bank[0][:, 0:384].rearrange("p (h e) -> p h e", h=4), ACT.Copy,
                           scale=stat[:, 2 * t:2 * t + 1])
                    kv = bank[1][:, :].rearrange("p (h e) -> p h e", h=4)
                    fn(qk_t[:, 1, :, 0:NOPE], kv[:, :, 0:NOPE], ACT.Copy, scale=stat[:, 2 * t + 1:2 * t + 2])
                    fn(v_a[:, t], kv[:, :, NOPE:P], ACT.Copy, scale=stat[:, 2 * t + 1:2 * t + 2]).then_inc(qk_ok.sem, 1)
                    act.wait_ge(*qss_ok.at(layer, t + 1))
                    ss = stat[:, 8 + 4 * n0:16]
                    fn(ss, ss, ACT.Sqrt, bias=eps, scale=1.0 / QK).then_inc(qrt_ok.sem, 1)
                    if t < tiles:
                        act.wait_ge(*qkt_p.at(layer, t + 1))
                        fn(qT_a[0:QK, :, t * P:(t + 1) * P], bank[2][0:QK, :].rearrange("p (h t) -> p h t", h=4), ACT.Copy
                           ).then_inc(qT_ok.sem, 1)
                pairs = [(t, h) for t in range(tiles) for h in range(HEADS)]
                for n, (t, h) in enumerate(pairs):
                    size = 512 if t < 2 else 256
                    act.wait_ge(*am_ok.at(layer, n + 1))
                    if n >= 2:
                        act.wait_ge(*at_p.at(layer, n - 1))
                    fn(pa[:, n % 2, 0:size], bank[5 + n % 2][:, 0:size], ACT.Exp, bias=stat[:, 16 + n % 2:17 + n % 2],
                       scale=QK ** -0.5, accum_out=asum[:, t % 2, h:h + 1]).then_inc(ae_ok.sem, 1)
                    if h == 0 and t >= 1:
                        turn_out(layer, t - 1)
                turn_out(layer, tiles - 1)

            def turn_out(layer, t):
                act.wait_ge(*ya_p.at(layer, t + 1))
                fn(Y[:, 2:4, t * P:(t + 1) * P], bank[4][:, 0:256].rearrange("p (c t) -> p c t", c=2), ACT.Copy
                   ).then_inc(yat_ok.sem, 1)

            def merge(layer):
                size = TOUT[layer] * P
                with act.Fori(0, 2) as i:
                    for at in range(16):
                        act.wait_ge(mgate_p.sem, i * 16 + (32 * layer + at + 1))
                        act.wait_ge(macc_ok.sem, two_before(i, at) + 33 * layer)
                        bias = par[:, layer, bass.ds(i * 16 + (R_BGATE + at // 8 * 8 + at % 8), 1)]
                        fn(sg_m[:, at % 2, 0:size], bank[at % 2][:, 0:size], ACT.Sigmoid, bias=bias
                           ).then_inc(mgate_a.sem, 1)

            def output_projection(layer):
                n = 0
                for g in range(2):
                    for s in range(len(row_groups(layer))):
                        for half in range(2):
                            n += 1
                            act.wait_ge(*gb_p.at(layer, n))
                            fn(gt_b[:, g, s, half * 512:(half + 1) * 512], bank[4 + n % 2][:, :], ACT.Copy
                               ).then_inc(gb_ok.sem, 1)

            def router_and_shared_expert(layer):
                tiles = TOUT[layer]
                size = tiles * P
                act.wait_ge(*r_p.at(layer, 1))
                fn(sc_r[:, 0:tiles, :].rearrange("p t e -> p (t e)"), bank[2][:, 0:tiles * NE], ACT.Sigmoid
                   ).then_inc(r_sc.sem, 1)
                for t in range(tiles):
                    act.wait_ge(*rb_p.at(layer, t + 1))
                    for half in range(2):
                        ins = fn(hrow[:, t, half * 512:(half + 1) * 512], bank[4 + half][:, :], ACT.Copy)
                    ins.then_inc(rb_ok.sem, 1)
                for j in range(2):
                    act.wait_ge(*sh_p.at(layer, j + 1))
                    fn(sg_sh[:, j, 0:size], bank[0][:, 0:size], ACT.Sigmoid).then_inc(sh_sig.sem, 1)

            def experts(layer):
                cap = CAPS[layer]
                e0 = layer * NE

                def input_of(g, j):
                    act.wait_ge(xt_p.sem, g * 4 + (j + e0 + 1))
                    fn(xT[:, j % 2, 4 * cap:8 * cap], bank[1][:, 0:4 * cap], ACT.Copy).then_inc(xt_a.sem, 1)

                def hidden_of(g, j):
                    act.wait_ge(h_p.sem, g * 4 + (j + e0 + 1))
                    fn(sig_a[:, j % 2, 0:2 * cap], bank[2 + j % 2][:, 0:2 * cap], ACT.Sigmoid).then_inc(h_sig.sem, 1)

                def output_of(g, j):
                    e = g * 4 + j
                    act.wait_ge(y_p.sem, e + (e0 + 1))
                    if layer or not isinstance(e, int) or e >= 1:
                        act.wait_ge(y_out.sem, e * 16 + 16 * e0)
                    fn(ysb[0:cap, 512:1024], bank[5][0:cap, :], ACT.Copy).then_inc(y_a_ok.sem, 1)

                def group(g, first=False, last=False):
                    for j in range(4):
                        hidden_of(g, j)
                        if not last or j < 3:
                            input_of(g, j + 1)
                        if not first or j >= 1:
                            output_of(g, j - 1)

                input_of(0, 0)
                group(0, first=True)
                with act.Fori(1, NE // 4 - 1) as g:
                    group(g)
                group(NE // 4 - 1, last=True)
                output_of(NE // 4 - 1, 3)

            def further_passes(layer):
                cap = CAPS[layer]
                w, used, scan, sel_s, tbl, idx, rows, xt, xte, h, sig, a, y, ye, sent = OV[layer]
                act.wait_ge(*rank_ok.at(layer, 1))
                most = act.value_load(cnt_i[0:1, :], min_val=0, max_val=NT * P)
                with act.Fori(1, PASSES) as q:
                    with act.If(most > q * cap):
                        with act.Fori(0, NE) as e:
                            n = (q - 1) * NE + e
                            act.wait_ge(xt, n + 1)
                            fn(xT[:, 0, 4 * cap:8 * cap], bank[1][:, 0:4 * cap], ACT.Copy).then_inc(xte, 1)
                            act.wait_ge(h, n + 1)
                            fn(sig_a[:, 0, 0:2 * cap], bank[2][:, 0:2 * cap], ACT.Sigmoid).then_inc(sig, 1)
                            act.wait_ge(y, n + 2)
                            fn(ysb[0:cap, 512:1024], bank[5][0:cap, :], ACT.Copy).then_inc(ye, 1)

            def combine(layer):
                act.wait_ge(*moe_done.at(layer, 1))
                act.wait_ge(*sh_ok.at(layer, 2 * TOUT[layer]))
                n = 0
                for t in range(TOUT[layer]):
                    for half in range(2):
                        if n >= 2:
                            act.wait_ge(*comb_used.at(layer, n - 1))
                        src = y_rows[t * P * TOPK:(t + 1) * P * TOPK, half * 512:(half + 1) * 512]
                        act.dma_start(comb[:, n % 2], src.rearrange("(p j) d -> p j d", j=TOPK)
                                      ).then_inc(comb_in[n % 2].sem, 16)
                        n += 1

            for layer in range(DEPTH):
                norm(layer, 0)
                input_projection(layer)
                gates(layer)
                pool_branch(layer)
                mlstm(layer)
                latent_attention(layer)
                merge(layer)
                output_projection(layer)
                norm(layer, 1)
                router_and_shared_expert(layer)
                experts(layer)
                further_passes(layer)
                combine(layer)
            act.wait_ge(res_ok, DEPTH)
            act.dma_start(out[0].rearrange("(t p) d -> p t d", p=P), res[:, 0:2, :]).then_inc(out_done, 16)
            act.wait_ge(out_done, 16)

        @block.gpsimd
        def _(pool):
            def gather(layer, slot, i, done):
                cap = CAPS[layer]
                pool.sem_inc(reached, 1)
                pool.indirect_dma_start(out=xg[0:cap, slot, :], out_offset=None, in_=h2_rows,
                                        in_offset=bass.IndirectOffsetOnAxis(ap=idx_g[i][0:cap], axis=0)
                                        ).then_inc(done, 16)

            def scatter(layer, i, done):
                cap = CAPS[layer]
                pool.sem_inc(reached, 1)
                pool.indirect_dma_start(out=y_rows, out_offset=bass.IndirectOffsetOnAxis(ap=idx_s[i][0:cap], axis=0),
                                        in_=ysb[0:cap, :], in_offset=None,
                                        bounds_check=TOUT[layer] * P * TOPK - 1, oob_is_err=False).then_inc(done, 16)

            for layer in range(DEPTH):
                if layer:
                    pool.wait_ge(res_ok, layer)
                for dst, src in ((b_gatebias, ml_gate_bias), (b_gqn, mla_g_qn), (b_gkn, mla_g_kn), (b_router, moe_b_router)):
                    pool.dma_start(dst, src[layer:layer + 1, :].broadcast_to([P, dst.shape[1]])).then_inc(in_row.sem, 16)
                pool.dma_start(inv_cnt, inv_count.rearrange("p (c t) -> p c t", c=2)).then_inc(in_cnt.sem, 16)
                for t in range(TOUT[layer]):
                    pool.wait_ge(*rb_ok.at(layer, t + 1))
                    pool.dma_start(h2_rows[t * P:(t + 1) * P, :], hrow[:, t, :]).then_inc(h2_out.sem, 16)
                pool.wait_ge(*h2_out.at(layer, 16 * TOUT[layer]))
                pool.wait_ge(*sh_ok.at(layer, 2 * TOUT[layer]))
                e0 = layer * NE

                def gather_of(g, j):
                    e = g * 4 + j
                    pool.wait_ge(idx_ok.sem, e + (e0 + 1))
                    if layer or not isinstance(e, int) or e >= 2:
                        pool.wait_ge(xt_p.sem, e + (e0 - 1))
                    gather(layer, j % 2, j % 4, rows_in[j % 2].sem)

                def scatter_of(g, j):
                    e = g * 4 + j
                    pool.wait_ge(y_v.sem, e + (e0 + 1))
                    pool.wait_ge(y_a_ok.sem, e + (e0 + 1))
                    scatter(layer, j % 4, y_out.sem)

                def group(g, first=False, last=False):
                    for j in range(4):
                        if not last or j < 2:
                            gather_of(g, j + 2)
                        if not first or j >= 1:
                            scatter_of(g, j - 1)

                gather_of(0, 0)
                gather_of(0, 1)
                group(0, first=True)
                with pool.Fori(1, NE // 4 - 1) as g:
                    group(g)
                group(NE // 4 - 1, last=True)
                scatter_of(NE // 4 - 1, 3)
                pool.wait_ge(*y_out.at(layer, 16 * NE))
                w, used, scan, sel_s, tbl, idx, rows, xt, xte, h, sig, a, y, ye, sent = OV[layer]
                most = pool.value_load(cnt_i[0:1, :], min_val=0, max_val=NT * P)
                with pool.Fori(1, PASSES) as q:
                    with pool.If(most > q * CAPS[layer]):
                        with pool.Fori(0, NE) as e:
                            n = (q - 1) * NE + e
                            pool.wait_ge(idx, n + 1)
                            gather(layer, 0, 0, rows)
                            pool.wait_ge(ye, n * 2 + 2)
                            scatter(layer, 0, sent)
                            pool.wait_ge(sent, n * 16 + 16)
                pool.memset(pool_mark, 0.0).then_inc(moe_done.sem, 1)


_INS = ['x', 'c', 'ctx', 'c_ctx', 'w_mod', 'b_mod', 'g_mix', 'g_ffn', 'w_in', 'ml_gate_bias', 'ml_head_gain',
        'mla_g_cq', 'mla_g_ckv', 'mla_w_uq', 'mla_w_ukv', 'mla_g_qn', 'mla_g_kn', 'pool_w', 'pool_scale', 'conv_w',
        'conv_b', 'w_gate', 'b_gate', 'w_branch', 'w_out', 'moe_w_router', 'moe_b_router', 'moe_w1', 'moe_w3',
        'moe_w2', 'moe_ws1', 'moe_ws3', 'moe_ws2']


def kernel(**inputs):
    import concourse.bacc as bacc
    from concourse.bass_utils import run_bass_kernel_spmd

    nc = bacc.Bacc("TRN2", target_bir_lowering=False, num_devices=1)
    consts, inv_count = constants()
    arrays = {f"in_{n}": np.ascontiguousarray(inputs[n]) for n in _INS}
    arrays |= {"in_consts": consts, "in_inv_count": inv_count}
    args = [nc.dram_tensor(n, a.shape, F32, kind="ExternalInput").ap() for n, a in arrays.items()]
    out = nc.dram_tensor("out", (1, SEQ, D), F32, kind="ExternalOutput").ap()
    build(nc, *args, out)
    r = run_bass_kernel_spmd(nc, [arrays], core_ids=[0])
    return r.results[0]["out"]
```
